# Optimizing a Trainium2 kernel written in Bass

```python
import jax
import jax.numpy as jnp
from jax import lax
import numpy as np

D_MODEL = 1024
BATCH = 1
SEQ = 256
DEPTH = 4

N_MIXERS = 3
N_A = (DEPTH + 2) // 3
N_B = (DEPTH + 1) // 3
N_C = DEPTH // 3
N_SUB = 3
D_FF = 2816
NORM_EPS = 1e-6

RWKV_N = 64
RWKV_H = D_MODEL // RWKV_N
LORA_DECAY = 64
LORA_ICLR = 64
LORA_VRES = 32
LORA_GATE = 128
RWKV_GN_EPS = 64e-5

RET_H = 4
RET_DK = D_MODEL // RET_H
RET_DV = 2 * RET_DK
RET_CHUNK = 128
ROPE_BASE = 10000.0
HEAD_NORM_EPS = 1e-5

LRU_WIDTH = 1280
LRU_H = 5
LRU_BW = LRU_WIDTH // LRU_H
CONV_W = 4
LRU_C = 8.0

kernel_name = 'hybrid_rwkv7_retnet_rglru_macaron_adaln'

def rms_norm(x, g):
    xf = x.astype(jnp.float32)
    return xf * lax.rsqrt(jnp.mean(xf * xf, axis=-1, keepdims=True) + NORM_EPS) * g

def head_norm(y, eps):
    yc = y - jnp.mean(y, axis=-1, keepdims=True)
    return yc * lax.rsqrt(jnp.mean(yc * yc, axis=-1, keepdims=True) + eps)

def swiglu(h, w_in, w_out):
    a, b = jnp.split(h @ w_in, 2, axis=-1)
    return (jax.nn.silu(a) * b) @ w_out

def token_shift(h):
    return jnp.pad(h, ((0, 0), (1, 0), (0, 0)))[:, :-1]

def sublayer_in(res, g_pre, shift, scale):
    return rms_norm(res, g_pre) * (1.0 + scale[:, None]) + shift[:, None]

def sublayer_out(res, y, g_post, gate, weight):
    return res + weight * gate[:, None] * rms_norm(y, g_post)

def wkv7_scan(r, w, k, v, a, b):
    bsz, _, nh, n = r.shape

    def step(S, inp):
        r_t, w_t, k_t, v_t, a_t, b_t = inp
        sa = jnp.einsum('bhvk,bhk->bhv', S, a_t)
        S = S * w_t[:, :, None, :] + sa[..., None] * b_t[:, :, None, :] + v_t[..., None] * k_t[:, :, None, :]
        return S, jnp.einsum('bhvk,bhk->bhv', S, r_t)

    xs = tuple(jnp.moveaxis(t.astype(jnp.float32), 1, 0) for t in (r, w, k, v, a, b))
    _, ys = lax.scan(step, jnp.zeros((bsz, nh, n, n), jnp.float32), xs)
    return jnp.moveaxis(ys, 0, 1)

def rwkv7_mix(h, v_first, mu, w_rkv, w0, w1, w2, a0, a1, a2, g1, g2, k_k, k_a, r_k, ln_w, ln_b, w_o, vres):
    bsz, t_len, d = h.shape
    dx = token_shift(h) - h
    xr, xw, xk, xv, xa, xg = (h + dx * mu[j] for j in range(6))
    r = xr @ w_rkv[0]
    k = xk @ w_rkv[1]
    v = xv @ w_rkv[2]
    decay = jnp.exp(-jnp.exp(-jax.nn.softplus(-(w0 + jnp.tanh(xw @ w1) @ w2)) - 0.5))
    a = jax.nn.sigmoid(a0 + (xa @ a1) @ a2)
    g = jax.nn.sigmoid(xg @ g1) @ g2
    if vres is None:
        v_first = v
    else:
        v0, v1, v2 = vres
        v = v + (v_first - v) * jax.nn.sigmoid(v0 + (xv @ v1) @ v2)
    heads = lambda t: t.reshape(bsz, t_len, RWKV_H, RWKV_N)
    kk = heads(k * k_k)
    kk = kk / jnp.maximum(jnp.sqrt(jnp.sum(kk * kk, axis=-1, keepdims=True)), 1e-12)
    k = heads(k * (1.0 + (a - 1.0) * k_a))
    r, v, a, decay = heads(r), heads(v), heads(a), heads(decay)
    y = wkv7_scan(r, decay, k, v, -kk, kk * a)
    y = head_norm(y, RWKV_GN_EPS).reshape(bsz, t_len, d) * ln_w + ln_b
    bonus = jnp.sum(r * k * r_k, axis=-1, keepdims=True) * v
    return ((y + bonus.reshape(bsz, t_len, d)) * g) @ w_o, v_first

def rotary(x, pos):
    half = x.shape[-1] // 2
    inv = 1.0 / (ROPE_BASE ** jnp.linspace(0.0, 1.0, half, dtype=jnp.float32))
    ang = pos.astype(jnp.float32)[..., None] * inv
    cos = jnp.cos(ang)[:, :, None, :]
    sin = jnp.sin(ang)[:, :, None, :]
    x1, x2 = x[..., :half], x[..., half:]
    return jnp.concatenate([x1 * cos - x2 * sin, x1 * sin + x2 * cos], axis=-1)

def retention_mix(h, pos, w_in, w_o):
    bsz, t_len, _ = h.shape
    n_chunks = t_len // RET_CHUNK
    qk = RET_H * RET_DK
    q, k, v, g = jnp.split(h @ w_in, [qk, 2 * qk, 2 * qk + RET_H * RET_DV], axis=-1)
    q = rotary(q.reshape(bsz, t_len, RET_H, RET_DK), pos).astype(jnp.float32)
    k = (rotary(k.reshape(bsz, t_len, RET_H, RET_DK), pos) * RET_DK ** -0.5).astype(jnp.float32)
    v = v.reshape(bsz, t_len, RET_H, RET_DV).astype(jnp.float32)
    log_gamma = jnp.log(1.0 - 2.0 ** (-5.0 - jnp.arange(RET_H, dtype=jnp.float32)))
    idx = jnp.arange(RET_CHUNK, dtype=jnp.float32)
    diff = idx[:, None] - idx[None, :]
    inner = jnp.where(diff >= 0, jnp.exp(log_gamma[:, None, None] * jnp.maximum(diff, 0.0)), 0.0)
    q_decay = jnp.exp(log_gamma[None, :] * (idx[:, None] + 1.0))[None, :, :, None]
    k_decay = jnp.exp(log_gamma[None, :] * (RET_CHUNK - 1.0 - idx[:, None]))[None, :, :, None]
    chunk_decay = jnp.exp(log_gamma * RET_CHUNK)[None, :, None, None]
    to_chunks = lambda t: jnp.moveaxis(t.reshape(bsz, n_chunks, RET_CHUNK, RET_H, -1), 1, 0)

    def step(R, inp):
        q_c, k_c, v_c = inp
        s = jnp.einsum('bihd,bjhd->bhij', q_c, k_c) * inner
        o = jnp.einsum('bhij,bjhe->bihe', s, v_c)
        o = o + jnp.einsum('bihd,bhde->bihe', q_c, R) * q_decay
        R = R * chunk_decay + jnp.einsum('bjhd,bjhe->bhde', k_c * k_decay, v_c)
        return R, o

    R0 = jnp.zeros((bsz, RET_H, RET_DK, RET_DV), jnp.float32)
    _, o = lax.scan(step, R0, (to_chunks(q), to_chunks(k), to_chunks(v)))
    o = jnp.moveaxis(o, 0, 1).reshape(bsz, t_len, RET_H, RET_DV)
    o = head_norm(o, HEAD_NORM_EPS).reshape(bsz, t_len, RET_H * RET_DV)
    return (jax.nn.silu(g) * o) @ w_o

def rglru_mix(h, w_in, conv_w, conv_b, gate_w, gate_b, lam, w_o):
    bsz, t_len, _ = h.shape
    gate_branch, xb = jnp.split(h @ w_in, 2, axis=-1)
    xc = lax.conv_general_dilated(
        xb.astype(jnp.float32), conv_w.astype(jnp.float32)[:, None, :],
        window_strides=(1,), padding=[(CONV_W - 1, 0)],
        dimension_numbers=('NWC', 'WIO', 'NWC'), feature_group_count=LRU_WIDTH) + conv_b
    xg = xc.reshape(bsz, t_len, LRU_H, LRU_BW)
    gates = jax.nn.sigmoid(jnp.einsum('bthi,ghij->gbthj', xg, gate_w) + gate_b[:, None, None])
    i_gate = gates[0].reshape(bsz, t_len, LRU_WIDTH)
    r_gate = gates[1].reshape(bsz, t_len, LRU_WIDTH)
    log_a = -LRU_C * r_gate * jax.nn.softplus(-lam)
    a = jnp.exp(log_a)
    u = jnp.sqrt(-jnp.expm1(2.0 * log_a)) * (i_gate * xc)

    def combine(left, right):
        a_l, u_l = left
        a_r, u_r = right
        return a_l * a_r, a_r * u_l + u_r

    _, hs = lax.associative_scan(combine, (a, u), axis=1)
    return (jax.nn.gelu(gate_branch) * hs) @ w_o

def setup_inputs(seed: int = 0) -> dict:
    key = jax.random.key(seed)
    ks = iter(jax.random.split(key, 40))
    nrm = lambda shape, fan_in, s=1.0: jax.random.normal(next(ks), shape, jnp.float32) * (s * fan_in ** -0.5)
    rnd = lambda shape, s: jax.random.normal(next(ks), shape, jnp.float32) * s
    unif = lambda shape, lo, hi: jax.random.uniform(next(ks), shape, jnp.float32, lo, hi)
    D, F = D_MODEL, D_FF
    x = jax.random.normal(next(ks), (BATCH, SEQ, D), jnp.float32)
    c = jax.random.normal(next(ks), (BATCH, D), jnp.float32)
    start = jax.random.randint(next(ks), (BATCH, 1), 0, 1024, dtype=jnp.int32)
    positions = (start + jnp.arange(SEQ, dtype=jnp.int32)[None, :]).astype(jnp.int32)
    ada_w = nrm((DEPTH, D, 3 * N_SUB * D), D, 0.5)
    ada_b = rnd((DEPTH, 3 * N_SUB * D), 0.01)
    norm_g = 1.0 + rnd((DEPTH, 2 * N_SUB, D), 0.05)
    ffn_w_in = nrm((DEPTH, 2, D, 2 * F), D)
    ffn_w_out = nrm((DEPTH, 2, F, D), F)
    rwkv_mu = unif((N_A, 6, D), 0.0, 1.0)
    rwkv_w_rkv = nrm((N_A, 3, D, D), D)
    rwkv_w0 = unif((N_A, D), -6.0, 0.0)
    rwkv_w1 = nrm((N_A, D, LORA_DECAY), D)
    rwkv_w2 = nrm((N_A, LORA_DECAY, D), LORA_DECAY, 0.1)
    rwkv_a0 = rnd((N_A, D), 0.1)
    rwkv_a1 = nrm((N_A, D, LORA_ICLR), D)
    rwkv_a2 = nrm((N_A, LORA_ICLR, D), LORA_ICLR, 0.1)
    rwkv_g1 = nrm((N_A, D, LORA_GATE), D)
    rwkv_g2 = nrm((N_A, LORA_GATE, D), LORA_GATE)
    rwkv_k_k = 0.85 + rnd((N_A, D), 0.05)
    rwkv_k_a = 1.0 + rnd((N_A, D), 0.05)
    rwkv_r_k = rnd((N_A, RWKV_H, RWKV_N), 0.1)
    rwkv_ln_w = 1.0 + rnd((N_A, D), 0.05)
    rwkv_ln_b = rnd((N_A, D), 0.01)
    rwkv_w_o = nrm((N_A, D, D), D)
    rwkv_v0 = 1.0 + rnd((N_A - 1, D), 0.1)
    rwkv_v1 = nrm((N_A - 1, D, LORA_VRES), D)
    rwkv_v2 = nrm((N_A - 1, LORA_VRES, D), LORA_VRES, 0.1)
    ret_w_in = nrm((N_B, D, 2 * RET_H * RET_DK + 2 * RET_H * RET_DV), D)
    ret_w_o = nrm((N_B, RET_H * RET_DV, D), RET_H * RET_DV)
    lru_w_in = nrm((N_C, D, 2 * LRU_WIDTH), D)
    lru_conv_w = nrm((N_C, CONV_W, LRU_WIDTH), CONV_W)
    lru_conv_b = rnd((N_C, LRU_WIDTH), 0.01)
    lru_gate_w = nrm((N_C, 2, LRU_H, LRU_BW, LRU_BW), LRU_BW)
    lru_gate_b = rnd((N_C, 2, LRU_H, LRU_BW), 0.01)
    rad = jnp.sqrt(unif((N_C, LRU_WIDTH), 0.81, 0.998))
    lru_lambda = jnp.log(rad) - jnp.log1p(-rad)
    lru_w_o = nrm((N_C, LRU_WIDTH, D), LRU_WIDTH)
    return {'x': x, 'c': c, 'positions': positions, 'ada_w': ada_w, 'ada_b': ada_b, 'norm_g': norm_g,
            'ffn_w_in': ffn_w_in, 'ffn_w_out': ffn_w_out,
            'rwkv_mu': rwkv_mu, 'rwkv_w_rkv': rwkv_w_rkv, 'rwkv_w0': rwkv_w0, 'rwkv_w1': rwkv_w1,
            'rwkv_w2': rwkv_w2, 'rwkv_a0': rwkv_a0, 'rwkv_a1': rwkv_a1, 'rwkv_a2': rwkv_a2,
            'rwkv_g1': rwkv_g1, 'rwkv_g2': rwkv_g2, 'rwkv_k_k': rwkv_k_k, 'rwkv_k_a': rwkv_k_a,
            'rwkv_r_k': rwkv_r_k, 'rwkv_ln_w': rwkv_ln_w, 'rwkv_ln_b': rwkv_ln_b, 'rwkv_w_o': rwkv_w_o,
            'rwkv_v0': rwkv_v0, 'rwkv_v1': rwkv_v1, 'rwkv_v2': rwkv_v2,
            'ret_w_in': ret_w_in, 'ret_w_o': ret_w_o,
            'lru_w_in': lru_w_in, 'lru_conv_w': lru_conv_w, 'lru_conv_b': lru_conv_b,
            'lru_gate_w': lru_gate_w, 'lru_gate_b': lru_gate_b, 'lru_lambda': lru_lambda, 'lru_w_o': lru_w_o}

def reference(x, c, positions, ada_w, ada_b, norm_g, ffn_w_in, ffn_w_out,
              rwkv_mu, rwkv_w_rkv, rwkv_w0, rwkv_w1, rwkv_w2, rwkv_a0, rwkv_a1, rwkv_a2,
              rwkv_g1, rwkv_g2, rwkv_k_k, rwkv_k_a, rwkv_r_k, rwkv_ln_w, rwkv_ln_b, rwkv_w_o,
              rwkv_v0, rwkv_v1, rwkv_v2,
              ret_w_in, ret_w_o,
              lru_w_in, lru_conv_w, lru_conv_b, lru_gate_w, lru_gate_b, lru_lambda, lru_w_o):
    res = x.astype(jnp.float32)
    cond = jax.nn.silu(c.astype(jnp.float32))
    v_first = None
    for i in range(DEPTH):
        mod = (cond @ ada_w[i] + ada_b[i]).reshape(cond.shape[0], 3 * N_SUB, -1)
        y = swiglu(sublayer_in(res, norm_g[i, 0], mod[:, 0], mod[:, 1]), ffn_w_in[i, 0], ffn_w_out[i, 0])
        res = sublayer_out(res, y, norm_g[i, 1], mod[:, 2], 0.5)
        hin = sublayer_in(res, norm_g[i, 2], mod[:, 3], mod[:, 4])
        kind, j = i % N_MIXERS, i // N_MIXERS
        if kind == 0:
            vres = None if j == 0 else (rwkv_v0[j - 1], rwkv_v1[j - 1], rwkv_v2[j - 1])
            y, v_first = rwkv7_mix(hin, v_first, rwkv_mu[j], rwkv_w_rkv[j], rwkv_w0[j], rwkv_w1[j], rwkv_w2[j],
                                   rwkv_a0[j], rwkv_a1[j], rwkv_a2[j], rwkv_g1[j], rwkv_g2[j],
                                   rwkv_k_k[j], rwkv_k_a[j], rwkv_r_k[j], rwkv_ln_w[j], rwkv_ln_b[j],
                                   rwkv_w_o[j], vres)
        elif kind == 1:
            y = retention_mix(hin, positions, ret_w_in[j], ret_w_o[j])
        else:
            y = rglru_mix(hin, lru_w_in[j], lru_conv_w[j], lru_conv_b[j], lru_gate_w[j], lru_gate_b[j],
                          lru_lambda[j], lru_w_o[j])
        res = sublayer_out(res, y, norm_g[i, 3], mod[:, 5], 1.0)
        y = swiglu(sublayer_in(res, norm_g[i, 4], mod[:, 6], mod[:, 7]), ffn_w_in[i, 1], ffn_w_out[i, 1])
        res = sublayer_out(res, y, norm_g[i, 5], mod[:, 8], 0.5)
    return res.astype(x.dtype)


_drawn_inputs = setup_inputs


def setup_inputs(seed=0):
    import zlib

    import numpy as np

    out = dict(_drawn_inputs(seed))
    spreads = {}
    factors = {'rwkv_w1': 8.0,
     'rwkv_w2': 8.0,
     'rwkv_a1': 2.872,
     'rwkv_ln_w': 2.671,
     'rwkv_ln_b': 32.707,
     'rwkv_v0': 185.896,
     'rwkv_v1': 53.04,
     'rwkv_v2': 52.976,
     'lru_conv_b': 8.0,
     'lru_gate_b': 49.042}
    for name, (base, spread) in spreads.items():
        noise = np.random.default_rng([zlib.crc32(name.encode()), seed]).standard_normal(out[name].shape)
        drawn = base * np.exp(spread * noise) if base else spread * noise
        out[name] = jnp.asarray(drawn.astype(out[name].dtype))
    for name, factor in factors.items():
        out[name] = (out[name] * factor).astype(out[name].dtype)
    return out
```

```python
from contextlib import ExitStack

import numpy as np

import concourse.bass as bass
from concourse import mybir

F32 = mybir.dt.float32
F32R = mybir.dt.float32r
I32 = mybir.dt.int32
ALU = mybir.AluOpType
ACT = mybir.ActivationFunctionType
AX = mybir.AxisListType

P = 128
T = 256
D = 1024
KC = D // P
FF = 2816
FJ = FF // P
DEPTH = 4
NORM_EPS = 1e-6

RH, RN = 16, 64
DECAY_RATE = float(np.exp(-0.5))
GN_EPS = 64e-5
HEAD_EPS = 1e-5
RET_H = 4
LW = 1280
LC = LW // P
CONV_W = 4

UNIT = 16 * P
HALF_K = FJ // 2
WOUT = HALF_K * P
LRU_OUT = LC * P

CONSTS = 16 * 10
ARENA = (2 * KC + 2 * FJ + 38) * T
ROUND = 1.5 * 2.0 ** 23
PI_LOW = 3.1415925
MU_AT = (3, 1, 2, 0, 4, 5)
LORA_AT = (0, 1, 2, 3)
WKV_MUL = ("m1t", "m13", "m24", "vt", "bt", "kt", "d2", "d2t", "t2", "d4", "d4t", "t3", "d8t", "t4", "n1", "n1t",
           "n2", "n3", "g", "h", "sa", "y", "ds")
WKV_VEC = ("begin", "lm", "r", "a", "b", "k_b", "dt", "ot", "d", "t1", "m3", "m2_b", "m4", "d2", "d2t", "t2", "d4t",
           "t3", "td", "n1", "e1", "n2", "e2", "e3", "g", "h", "sa", "sum", "state")
WKV_ACT = ("ep", "en", "em", "v_b", "a_b", "b_b", "d_b", "dt_b", "ot_b", "vt_b", "vt_s", "bt_b", "kt_b", "d2_b",
           "d2t_b", "d4_b", "d4t_b", "d8t_b", "td_b", "n1t_b", "e_b", "sa_b", "y", "st_b")
PLAN = [(l, s) for l in range(DEPTH) for s in range(3)]
LN_EXP = "natural_log_exp_and_others"


def kind_of(layer, sub):
    return "ffn" if sub != 1 else ("rwkv", "ret", "lru")[layer % 3]


UNITS = {"ffn": [UNIT] * FJ + [WOUT] * 16, "rwkv": [UNIT] * 20, "ret": [UNIT] * 32,
         "lru": [UNIT] * 13 + [LRU_OUT] * 8}
USES = {"ffn": FJ + 8, "rwkv": 34, "ret": 32, "lru": 28}


class Step:

    def __init__(self, base, i=None, stride=2):
        self.base, self.i, self.stride = base, i, stride

    def __add__(self, k):
        return Step(self.base + k, self.i, self.stride)

    def count(self, k=0):
        n = self.base + k
        return n if self.i is None else self.i * self.stride + n

    @property
    def slot(self):
        return self.base % 2

    def landed(self):
        n = 16 * (self.base // 2 + 1)
        return n if self.i is None else self.i * (8 * self.stride) + n


class Tally:

    def __init__(self, eng, sem):
        self.eng, self.sem, self.n, self.turn = eng, sem, 0, None

    def up(self, ins):
        ins.then_inc(self.sem, 1)
        self.n += 1

    def settle(self):
        self.eng.wait_ge(self.sem, self.n if self.turn is None else self.turn + self.n)

    def loop(self, times, per):
        with self.eng.Fori(0, times) as i:
            start = self.n
            self.turn = i * per
            yield i
            assert self.n - start == per, (self.n - start, per)
        self.turn, self.n = None, start + times * per


def build_program(nc, x_t, c_row, ada_t, ada_bt, norm_gt, w_in, w_out, pos_row, rope_freq, ret_decay, ident_c, ret_w,
                  ret_wo, lru_w, lru_wo, rwkv_w, rwkv_par, wkv_const, lru_par, v_keep, out):
    ctx = ExitStack()
    with ctx:
        def sb(name, shape, dt=F32):
            return ctx.enter_context(nc.sbuf_tensor(name, shape, dt))

        def pb(name, shape):
            return ctx.enter_context(nc.psum_tensor(name, shape, F32))

        def sem(name):
            return ctx.enter_context(nc.semaphore(name))

        res = sb("res", [P, KC, T])
        hn = sb("hn", [P, KC, T + 1])
        ysq = sb("ysq", [P, 2 * KC, T])
        ybuf = ysq[:, 0:KC, :]
        sq = ysq[:, KC:2 * KC, :]
        raw_w = sb("raw_w", [P, 2, UNIT])
        wt_hi = sb("wt_hi", [P, 2, UNIT], F32R)
        wt_lo = sb("wt_lo", [P, 2, UNIT], F32R)
        ada_w = sb("ada_w", [P, 2, D])
        cond = sb("cond", [P, D])
        ones = sb("ones", [P, P])
        eps = sb("eps", [P, 4])
        rstd = sb("rstd", [P, 2, T])
        scaled = sb("scaled", [P, 2, T])
        mod_acc = sb("mod_acc", [P, 2])
        mod = sb("mod", [P, 24])
        coef = sb("coef", [P, 2, 24])
        ada_b = sb("ada_b", [P, DEPTH * 72])
        norm_g = sb("norm_g", [P, DEPTH * 48])
        gate_act = sb("gate_act", [P, 2, T])
        h_raw = scaled
        ident = sb("ident", [P, P])
        cos_t = sb("cos_t", [P, T])
        sin_t = sb("sin_t", [P, T])
        freq = sb("freq", [P, 1])
        with nc.sbuf_tensor("x_hi", [P, KC, T], F32R) as x_hi, nc.sbuf_tensor("x_lo", [P, KC, T], F32R) as x_lo:
            with nc.sbuf_tensor("h_hi", [P, FJ, T], F32R) as h_hi, nc.sbuf_tensor("h_lo", [P, FJ, T], F32R) as h_lo:
                pass
        arena = sb("arena", [P, ARENA])
        at_h_hi = 2 * KC * T
        at_h_lo = at_h_hi + FJ * T
        above_h = at_h_lo + FJ * T

        def view(at, *shape):
            n = int(np.prod(shape))
            assert at + n <= ARENA
            v = arena[:, at:at + n]
            return v if len(shape) == 1 else v.rearrange("p (a b) -> p a b", a=shape[0]) if len(shape) == 2 else \
                v.rearrange("p (a b c) -> p a b c", a=shape[0], b=shape[1])

        ret_v = view(above_h, 2, 2 * D)
        ret_g = view(above_h + 4096, 16, T)
        ret_s = view(above_h + 8192, RET_H, 384)
        ret_o = view(at_h_lo + 16 * T, 2, 512)
        lru_gb = view(above_h, LC, T)
        lru_xb = view(above_h + LC * T, LC, T + 3)
        lru_rg = view(above_h + LC * T, LC, T)
        lru_xc = view(above_h + LC * (2 * T + 3), LC, T)
        lru_ig = ysq[:, 0:LC, :]
        lru_p = sb("lru_p", [P, 8 * LC])
        lru_c = sb("lru_c", [P, 6, LC])
        stats = sb("stats", [P, 2, 6])
        mv = sb("mv", [P, 2, 2])
        lru_t = view(at_h_hi + LC * T, LC, T)
        lru_d = view(at_h_lo + LC * T, LC, T)
        ret_mv = sb("ret_mv", [P, 2, 8])
        ret_rs = sb("ret_rs", [P, 8])

        rk_v, rk_k, rk_r, rk_w = (view(above_h + n * KC * T, KC, T) for n in range(4))
        rk_a = view(at_h_hi, KC, T)
        rk_g = view(at_h_hi + KC * T, KC, T)
        rk_sv = view(at_h_lo, KC, T)
        rk_bonus = view(at_h_lo + KC * T, KC, T)
        rk_kk = hn[:, :, 1:T + 1]
        rk_l = sq
        lora_raw = view(above_h + 32 * T, 4, T)
        free = iter([0, 2, 4, 6, 8, 10, 12, 14] + [32, 34, 36, 38, 40, 42, 44] + [54, 56, 58] + [94, 96])
        spots = [n * T for n in free]

        def stacked(n, w=64):
            return view(n, 4, w)

        a_b, b_b, k_b, v_b, d_b, dt_b, ot_b, m2_b = (stacked(n, P) for n in spots[:8])
        bt_b, kt_b, vt_b = (stacked(n, P) for n in spots[8:11])
        st_b = [stacked(n, P) for n in spots[11:13]]
        ar_s, m3_s, m4_s = stacked(spots[13], P), stacked(spots[14]), stacked(spots[14] + T)
        b_s, ot_s = stacked(spots[15]), stacked(spots[15] + T)
        vt_s, sa_s = stacked(spots[16]), stacked(spots[16] + T)
        t_s, e_s = stacked(spots[17]), stacked(spots[17] + T)
        wkv_c = sb("wkv_c", [P, 10, 64])
        d_s, dt_s, d2_s, d2t_s, n2_s, lm_s = (ybuf[:, n, :].rearrange("p (a b) -> p a b", a=4) for n in range(6))
        ep_s = view(spots[19], 4, 64)
        en_s = view(spots[19] + T, 4, 64)
        em_s = ybuf[:, 6, :].rearrange("p (a b) -> p a b", a=4)
        g_s = ybuf[:, 7, :].rearrange("p (a b) -> p a b", a=4)
        d2_b, d8t_b, sa_b = b_b, b_b, b_b
        d2t_b, td_b = k_b, k_b
        d4_b, n1t_b = v_b, v_b
        d4t_b, e_b = d_b, d_b
        d4t_s, n1_s, h_s = d_s, dt_s, d2t_s
        st_s = [stacked(92 * T), stacked(93 * T)]
        rk_p = sb("rk_p", [P, 2, 112])
        head_ones = sb("head_ones", [P, P])

        out_ps = pb("out_ps", [P, 2, 512])
        sum_ps = pb("sum_ps", [P, 512])
        mix_ps = pb("mix_ps", [P, 5, 512])
        wkv_ps = [mix_ps[:, n, :] for n in range(5)] + [out_ps[:, n, :] for n in range(2)]

        consts_in = sem("consts_in")
        const_set = sem("const_set")
        cond_done = sem("cond_done")
        unit_in = [sem("unit_in0"), sem("unit_in1")]
        hi_done = sem("hi_done")
        lo_done = sem("lo_done")
        unit_mul = sem("unit_mul")
        out_taken = sem("out_taken")
        ada_in = [sem("ada_in0"), sem("ada_in1")]
        ada_used = sem("ada_used")
        sq_ready = sem("sq_ready")
        sum_done = sem("sum_done")
        rs_ready = sem("rs_ready")
        res_ready = sem("res_ready")
        hn_ready = sem("hn_ready")
        xh_ready = sem("xh_ready")
        x_ready = sem("x_ready")
        y_ready = sem("y_ready")
        silu_done = sem("silu_done")
        h_ready = sem("h_ready")
        hh_ready = sem("hh_ready")
        hl_ready = sem("hl_ready")
        vec_own = sem("vec_own")
        act_own = sem("act_own")
        stored = sem("stored")
        rope_arg = sem("rope_arg")
        rope_done = sem("rope_done")
        kq_ready = sem("kq_ready")
        v_ready = sem("v_ready")
        g_ready = sem("g_ready")
        score_mul = sem("score_mul")
        score_ready = sem("score_ready")
        decay_in = sem("decay_in")
        o_mul = sem("o_mul")
        var_ready = sem("var_ready")
        o_ready = sem("o_ready")
        turned = sem("turned")
        r_ready = sem("r_ready")
        rh_ready = sem("rh_ready")
        rl_ready = sem("rl_ready")
        lru_par_in = sem("lru_par_in")
        lam_exp = sem("lam_exp")
        lam_abs = sem("lam_abs")
        xb_ready = sem("xb_ready")
        gb_ready = sem("gb_ready")
        conv_ready = sem("conv_ready")
        xch_ready = sem("xch_ready")
        xcl_ready = sem("xcl_ready")
        gate_ready = sem("gate_ready")
        tanh_ready = sem("tanh_ready")
        a_ready = sem("a_ready")
        m_ready = sem("m_ready")
        beta_ready = sem("beta_ready")
        dx_ready = sem("dx_ready")
        xj_raw = sem("xj_raw")
        xj_hi = sem("xj_hi")
        xj_ready = sem("xj_ready")
        proj_read = sem("proj_read")
        lora_mul = sem("lora_mul")
        lora_out = sem("lora_out")
        lora_hi = sem("lora_hi")
        lora_ready = sem("lora_ready")
        v_kept = sem("v_kept")
        v_back = sem("v_back")
        kk_sq = sem("kk_sq")
        kk_in = sem("kk_in")
        head_sum = sem("head_sum")
        kk_norm = sem("kk_norm")
        kk_root = sem("kk_root")
        rk_prod = sem("rk_prod")
        wkv_mul = sem("wkv_mul")
        wkv_vec = sem("wkv_vec")
        wkv_act = sem("wkv_act")
        turn_over = sem("turn_over")
        yc_ready = sem("yc_ready")
        yc_sq = sem("yc_sq")
        y_rs = sem("y_rs")
        yg_ready = sem("yg_ready")
        yg_hi = sem("yg_hi")
        yg_lo = sem("yg_lo")
        rs_ready_o = sem("rs_ready_o")
        lru_pad = sem("lru_pad")
        gate_mul = sem("gate_mul")
        hs_ready = sem("hs_ready")
        hsh_ready = sem("hsh_ready")
        hsl_ready = sem("hsl_ready")

        block = ctx.enter_context(nc.Block())
        n_sub = len(PLAN)
        kinds = [kind_of(*p) for p in PLAN]
        widths = [w for k in kinds for w in UNITS[k]]
        uses = [sum(USES[k] for k in kinds[:s]) for s in range(n_sub)]

        def width(u):
            return widths[u] if u < len(widths) else None

        def ffn_index(s):
            return sum(k == "ffn" for k in kinds[:s])

        def plain_index(s):
            return sum(k != "rwkv" for k in kinds[:s])

        def rwkv_index(s):
            return sum(k == "rwkv" for k in kinds[:s])

        def reads_before(s):
            return sum(26 + 4 * (PLAN[n][0] > 0) for n in range(s) if kinds[n] == "rwkv")

        def lora_before(s):
            return sum(12 + 4 * (PLAN[n][0] > 0) for n in range(s) if kinds[n] == "rwkv")

        def mixed_x(j):
            n = (0, 1, 2, 0, 1, 2)[j]
            return (x_hi, x_lo) if n == 0 else (h_hi[:, 8 * n - 8:8 * n, :], h_lo[:, 8 * n - 8:8 * n, :])

        def head_ps(m):
            return mix_ps[:, m // 2, m % 2 * T:m % 2 * T + T]

        def part(bank, n):
            return wkv_ps[bank][:, n * T:n * T + T].rearrange("p (a b) -> p a b", a=4)

        def wkv_count(order, s, it, name):
            n = order.index(name) + 1 + rwkv_index(s) * 8 * len(order)
            return it * len(order) + n

        @block.sync
        def _(sp):
            sp.dma_start(res[:, :, :], x_t).then_inc(consts_in, 16)
            sp.dma_start(ada_b[:, :], ada_bt).then_inc(consts_in, 16)
            sp.dma_start(norm_g[:, :], norm_gt).then_inc(consts_in, 16)
            sp.dma_start(cond[:, :], c_row.partition_broadcast(P)).then_inc(consts_in, 16)
            sp.dma_start(freq[:, :], rope_freq).then_inc(consts_in, 16)
            sp.dma_start(ident[:, :], ident_c).then_inc(consts_in, 16)
            sp.dma_start(sq[:, 0, :].bitcast(I32), pos_row.partition_broadcast(P)).then_inc(consts_in, 16)
            sp.dma_start(lru_p[:, :], lru_par).then_inc(consts_in, 16)
            sp.dma_start(rk_p[:, :, :], rwkv_par).then_inc(consts_in, 16)
            sp.dma_start(wkv_c[:, :, :], wkv_const).then_inc(consts_in, 16)

            def load(step, src, w, free=True):
                if free:
                    sp.wait_ge(lo_done, step.count(-1))
                sp.dma_start(raw_w[:, step.slot, 0:w], src).then_inc(unit_in[step.slot], 16)

            def stream(u, src, n, w):
                k = 0
                while k < n and (u + k < 2 or (n - k) % 2):
                    load(Step(u + k), src[k], w, u + k >= 2)
                    k += 1
                if k < n:
                    with sp.Fori(0, (n - k) // 2) as i:
                        for b in range(2):
                            load(Step(u + k + b, i), src[i * 2 + (k + b)], w)
                return u + n

            u = 0
            for s, (layer, sub) in enumerate(PLAN):
                if kinds[s] == "ffn":
                    f = layer * 2 + sub // 2
                    u = stream(u, w_in[f], FJ, UNIT)
                    u = stream(u, w_out[f], 16, WOUT)
                elif kinds[s] == "ret":
                    u = stream(u, ret_w, 24, UNIT)
                    u = stream(u, ret_wo, 8, UNIT)
                elif kinds[s] == "rwkv":
                    u = stream(u, rwkv_w[layer // 3], 20, UNIT)
                elif kinds[s] == "lru":
                    u = stream(u, lru_w, 13, UNIT)
                    u = stream(u, lru_wo, 8, LRU_OUT)
            for m in range(KC):
                sp.wait_ge(res_ready, 8 * (n_sub - 1) + m + 1)
                sp.dma_start(out[:, m, :], res[:, m, :]).then_inc(stored, 16)
            sp.wait_ge(stored, 16 * KC)

        @block.gpsimd
        def _(pool):
            for s, (layer, sub) in enumerate(PLAN):
                src = ada_t[layer * 72 + sub * 24:layer * 72 + sub * 24 + 24]
                a = 24 * s
                first = 0
                if s == 0:
                    for k in range(2):
                        pool.dma_start(ada_w[:, k, :], src[k]).then_inc(ada_in[k], 16)
                    first = 1
                with pool.Fori(first, 12) as i:
                    for b in range(2):
                        pool.wait_ge(ada_used, Step(a + b, i).count(-1))
                        pool.dma_start(ada_w[:, b, :], src[i * 2 + b]).then_inc(ada_in[b], 16)

        @block.scalar
        def _(act):
            own = Tally(act, act_own)

            def split_hi(step, w):
                if w is None:
                    return
                act.wait_ge(unit_in[step.slot], step.landed())
                if step.base >= 2:
                    act.wait_ge(unit_mul, step.count(-1))
                nc.scalar.activation(wt_hi[:, step.slot, 0:w], raw_w[:, step.slot, 0:w], ACT.Copy).then_inc(hi_done, 1)

            def inverse_rms(n):
                act.wait_ge(sum_done, n + 1)
                own.up(nc.scalar.activation(rstd[:, n % 2, :], sum_ps[:, 0:T], ACT.Ln, bias=eps[:, 0:1], scale=1.0 / D))
                own.settle()
                nc.scalar.activation(rstd[:, n % 2, :], rstd[:, n % 2, :], ACT.Exp, scale=-0.5).then_inc(rs_ready, 1)

            def pre_norm(s):
                nc.scalar.preload_act_table_set(LN_EXP)
                for m in range(KC):
                    if s:
                        act.wait_ge(res_ready, 8 * (s - 1) + m + 1)
                        act.wait_ge(sum_done, 2 * s)
                    nc.scalar.activation(sq[:, m, :], res[:, m, :], ACT.Square).then_inc(sq_ready, 1)
                inverse_rms(2 * s)

            def round_x(s):
                for m in range(KC):
                    act.wait_ge(hn_ready, 8 * s + m + 1)
                    nc.scalar.activation(x_hi[:, m, :], hn[:, m, 1:T + 1], ACT.Copy).then_inc(xh_ready, 1)

            def square_y(s, m):
                if isinstance(m, int):
                    act.wait_ge(y_ready, 8 * s + m + 1)
                else:
                    act.wait_ge(y_ready, m + (8 * s + 1))
                nc.scalar.activation(sq[:, bass.ds(m, 1), :], ybuf[:, bass.ds(m, 1), :], ACT.Square).then_inc(sq_ready, 1)

            def ffn(s, u):
                f = ffn_index(s)
                pre_norm(s)
                round_x(s)
                nc.scalar.preload_act_table(ACT.Silu)

                def pair(step, j, w0, w1):
                    for b, w in ((0, w0), (1, w1)):
                        split_hi(step + (2 + b), w)
                        act.wait_ge(unit_mul, (step + b).count(1))
                        if not (isinstance(j, int) and j + b < 2 and f == 0):
                            act.wait_ge(h_ready, j + (FJ * f + b - 1))
                        sl = (step + b).slot
                        nc.scalar.activation(gate_act[:, sl, :], out_ps[:, bank0 ^ b, 0:T], ACT.Silu).then_inc(silu_done, 1)
                        act.wait_ge(h_ready, j + (FJ * f + b + 1))
                        nc.scalar.activation(h_hi[:, bass.ds(j + b, 1), :], h_raw[:, sl:sl + 1, :], ACT.Copy).then_inc(hh_ready, 1)

                bank0 = uses[s] % 2
                pair(Step(u), 0, UNIT, UNIT)
                with act.Fori(1, FJ // 2 - 1) as i:
                    pair(Step(u, i), i * 2, UNIT, UNIT)
                pair(Step(u + FJ - 2), FJ - 2, WOUT, WOUT)
                v = u + FJ
                nc.scalar.preload_act_table_set(LN_EXP)

                def quad(step, m, last=False):
                    for b in range(2):
                        for g in range(2):
                            k = 2 * b + g
                            split_hi(step + (2 + k), width(v + 16 + k - 2) if last and k >= 2 else WOUT)
                        square_y(s, m + b)

                with act.Fori(0, 3) as i:
                    quad(Step(v, i, 4), i * 2)
                quad(Step(v + 12), 6, True)
                inverse_rms(2 * s + 1)

            def out_proj(s, u, w):
                n = u + 8

                def two(step, m, w0, w1):
                    for b, wb in ((0, w0), (1, w1)):
                        split_hi(step + (2 + b), wb)
                        square_y(s, m + b)

                with act.Fori(0, 3) as i:
                    two(Step(u, i), i * 2, w, w)
                two(Step(u + 6), 6, width(n), width(n + 1))
                inverse_rms(2 * s + 1)

            def retention(s, u):
                pre_norm(s)
                round_x(s)
                act.dma_start(ret_s, ret_decay).then_inc(decay_in, 16)
                nc.scalar.preload_act_table(ACT.Silu)
                with act.Fori(0, 4) as i:
                    for b in range(2):
                        split_hi(Step(u + 2 + b, i), UNIT)
                v = u + 8
                with act.Fori(0, 4) as i:
                    for b in range(2):
                        split_hi(Step(v + 2 + b, i), UNIT)
                        act.wait_ge(unit_mul, Step(v + b, i).count(1))
                        nc.scalar.activation(ret_v.rearrange("p t (j e) -> p j t e", e=T)[:, bass.ds(i * 2 + b, 1)],
                                             out_ps[:, (uses[s] + b) % 2:(uses[s] + b) % 2 + 1, :].rearrange("p o (t e) -> p o t e", t=2),
                                             ACT.Copy).then_inc(v_ready, 1)
                g = v + 8
                for i in range(8):
                    split_hi(Step(g + i + 2), width(g + i + 2))
                    act.wait_ge(unit_mul, g + i + 1)
                    nc.scalar.activation(ret_g[:, 2 * i:2 * i + 2, :], out_ps[:, (uses[s] + i) % 2, :].rearrange("p (c t) -> p c t", c=2),
                                         ACT.Silu).then_inc(g_ready, 1)
                    if i == 4:
                        act.wait_ge(var_ready, 8)
                        own.up(nc.scalar.activation(ret_rs[:, :], ret_mv[:, 1, :], ACT.Ln, bias=eps[:, 2:3]))
                        own.settle()
                        nc.scalar.activation(ret_rs[:, :], ret_rs[:, :], ACT.Exp, scale=-0.5).then_inc(rs_ready_o, 1)
                    if i > 4:
                        ret_round(2 * (i - 5))
                        ret_round(2 * (i - 5) + 1)
                ret_round(6)
                ret_round(7)
                nc.scalar.preload_act_table_set(LN_EXP)
                out_proj(s, g + 8, UNIT)

            def ret_round(n):
                h, t = n // 2, n % 2
                act.wait_ge(r_ready, n + 1)
                nc.scalar.activation(h_hi[:, 4 * h:4 * h + 4, t * P:t * P + P],
                                     ret_o[:, t, :].rearrange("p (c t) -> p c t", c=4), ACT.Copy).then_inc(rh_ready, 1)

            def lru(s, u):
                q = uses[s]
                pre_norm(s)
                round_x(s)
                for i in range(5):
                    split_hi(Step(u + i + 2), UNIT)
                    act.wait_ge(unit_mul, u + i + 1)
                    if i == 0:
                        act.wait_ge(lru_pad, 1)
                    nc.scalar.activation(lru_xb[:, 2 * i:2 * i + 2, 3:T + 3], out_ps[:, (q + i) % 2, :].rearrange("p (c t) -> p c t", c=2),
                                         ACT.Copy).then_inc(xb_ready, 1)
                nc.scalar.preload_act_table(ACT.Gelu_apprx_tanh)
                for i in range(5, 10):
                    split_hi(Step(u + i + 2), UNIT)
                    act.wait_ge(unit_mul, u + i + 1)
                    c = 2 * (i - 5)
                    nc.scalar.activation(lru_gb[:, c:c + 2, :], out_ps[:, (q + i) % 2, :].rearrange("p (c t) -> p c t", c=2),
                                         ACT.Gelu_apprx_tanh).then_inc(gb_ready, 1)
                    for m in (c, c + 1):
                        act.wait_ge(conv_ready, m + 1)
                        nc.scalar.activation(h_hi[:, m, :], lru_xc[:, m, :], ACT.Copy).then_inc(xch_ready, 1)
                nc.scalar.preload_act_table(ACT.Sigmoid)
                for w in range(10):
                    h, g = w // 2, w % 2
                    act.wait_ge(gate_mul, w + 1)
                    for c in range(2):
                        m = 2 * h + c
                        dst = (lru_ig, lru_rg)[g][:, m, :]
                        nc.scalar.activation(dst, out_ps[:, (q + 10 + w) % 2, c * T:c * T + T], ACT.Sigmoid,
                                             bias=lru_p[:, 50 + 10 * g + m:51 + 10 * g + m]).then_inc(gate_ready, 1)
                    if g:
                        act.wait_ge(gate_ready, 2 * w + 2)
                        for m in (2 * h, 2 * h + 1):
                            nc.scalar.activation(lru_t[:, m, :], lru_rg[:, m, :], ACT.Tanh, scale=lru_c[:, 0, m:m + 1]).then_inc(tanh_ready, 1)
                    if w % 4 == 3 or w == 9:
                        split_hi(Step(u + 12 + w // 4), width(u + 12 + w // 4))
                nc.scalar.preload_act_table(ACT.Exp)
                act.wait_ge(tanh_ready, LC)
                for m in range(LC):
                    nc.scalar.activation(lru_rg[:, m, :], lru_rg[:, m, :], ACT.Exp, scale=lru_c[:, 1, m:m + 1]).then_inc(a_ready, 1)
                nc.scalar.preload_act_table(ACT.Sqrt)
                for h in range(5):
                    act.wait_ge(m_ready, h + 1)
                    nc.scalar.activation(lru_t[:, 2 * h:2 * h + 2, :], lru_t[:, 2 * h:2 * h + 2, :], ACT.Sqrt).then_inc(beta_ready, 1)
                for h in range(5):
                    act.wait_ge(hs_ready, h + 1)
                    nc.scalar.activation(h_hi[:, 2 * h:2 * h + 2, :], lru_xc[:, 2 * h:2 * h + 2, :], ACT.Copy).then_inc(hsh_ready, 1)
                nc.scalar.preload_act_table_set(LN_EXP)
                out_proj(s, u + 13, LRU_OUT)

            def rwkv(s, u):
                layer = PLAN[s][0]
                q, ri, vres = uses[s], rwkv_index(s), layer > 0
                rd0, par = reads_before(s), rk_p[:, layer // 3, :]
                n_raw = [48 * ri]

                def round_mixed(count):
                    for _ in range(count):
                        n = n_raw[0]
                        j, m = n % 48 // 8, n % 8
                        act.wait_ge(xj_raw, n + 1)
                        nc.scalar.activation(mixed_x(j)[0][:, m, :], scaled[:, n % 2, :], ACT.Copy).then_inc(xj_hi, 1)
                        n_raw[0] += 1

                def read(bank, dst, func, bias=None):
                    src = out_ps[:, bank % 2, :].rearrange("p (c t) -> p c t", c=2)
                    if bias is None:
                        ins = nc.scalar.activation(dst, src, func)
                    else:
                        for c in range(2):
                            ins = nc.scalar.activation(dst[:, c, :], src[:, c, :], func, bias=bias[:, c:c + 1])
                    ins.then_inc(proj_read, 1)

                def lora_round(js):
                    for j in js:
                        act.wait_ge(lora_out, 4 * ri + j + 1)
                        nc.scalar.activation(h_hi[:, 16 + LORA_AT[j], :], lora_raw[:, LORA_AT[j], :], ACT.Copy).then_inc(lora_hi, 1)

                pre_norm(s)
                if vres:
                    act.wait_ge(v_kept, 16)
                    act.dma_start(ybuf, v_keep).then_inc(v_back, 16)
                nc.scalar.preload_act_table(ACT.Sigmoid)
                round_mixed(8)
                for i in range(4):
                    split_hi(Step(u + i + 2), UNIT)
                    act.wait_ge(unit_mul, u + i + 1)
                    read(q + i, rk_v[:, 2 * i:2 * i + 2, :], ACT.Copy)
                    round_mixed(4)
                if not vres:
                    act.wait_ge(proj_read, rd0 + 4)
                    act.dma_start(v_keep, rk_v).then_inc(v_kept, 16)
                split_hi(Step(u + 6), UNIT)
                act.wait_ge(unit_mul, u + 5)
                nc.scalar.activation(lora_raw[:, 0, :], out_ps[:, (q + 4) % 2, 0:T] if vres else out_ps[:, (q + 4) % 2, T:2 * T], ACT.Copy).then_inc(lora_out, 1)
                nc.scalar.activation(lora_raw[:, 1, :], out_ps[:, (q + 4) % 2, T:2 * T], ACT.Tanh).then_inc(lora_out, 1)
                act.wait_ge(lora_out, 4 * ri + 2)
                act.sem_inc(proj_read, 1)
                lora_round((0, 1))
                for i in range(5, 9):
                    split_hi(Step(u + i + 2), UNIT)
                    act.wait_ge(unit_mul, u + i + 1)
                    read(q + i, rk_k[:, 2 * i - 10:2 * i - 8, :], ACT.Copy)
                    round_mixed(4)
                for i in range(9, 13):
                    split_hi(Step(u + i + 2), UNIT)
                    act.wait_ge(unit_mul, u + i + 1)
                    read(q + i, rk_r[:, 2 * i - 18:2 * i - 16, :], ACT.Copy)
                    round_mixed(2)
                split_hi(Step(u + 15), UNIT)
                act.wait_ge(unit_mul, u + 14)
                nc.scalar.activation(lora_raw[:, 2, :], out_ps[:, (q + 13) % 2, 0:T], ACT.Copy).then_inc(lora_out, 1)
                nc.scalar.activation(lora_raw[:, 3, :], out_ps[:, (q + 13) % 2, T:2 * T], ACT.Sigmoid).then_inc(lora_out, 1)
                act.wait_ge(lora_out, 4 * ri + 4)
                act.sem_inc(proj_read, 1)
                lora_round((2, 3))
                n = 0
                for dst, bias in ((rk_w, 0), (rk_a, 8), (rk_g, None)) + (((rk_sv, 16),) if vres else ()):
                    for c in range(4):
                        act.wait_ge(lora_mul, lora_before(s) + n + 1)
                        read(q + 14 + n, dst[:, 2 * c:2 * c + 2, :], ACT.Copy if bias is None else ACT.Sigmoid,
                             None if bias is None else par[:, bias + 2 * c:bias + 2 * c + 2])
                        n += 1
                    if dst is rk_a:
                        split_hi(Step(u + 16), UNIT)
                split_hi(Step(u + 17), UNIT)
                nc.scalar.preload_act_table(ACT.Sqrt)
                act.wait_ge(kk_in, ri + 1)
                nc.scalar.activation(rk_bonus, rk_kk, ACT.Square).then_inc(kk_sq, 1)
                act.wait_ge(kk_norm, ri + 1)
                nc.scalar.activation(rk_bonus, rk_bonus, ACT.Sqrt).then_inc(kk_root, 1)
                nc.scalar.preload_act_table(ACT.Exp)
                wkv_scalar(s)
                nc.scalar.preload_act_table_set(LN_EXP)
                for m in range(KC):
                    act.wait_ge(yc_ready, 8 * ri + m + 1)
                    nc.scalar.activation(rk_w[:, m, :], rk_k[:, m, :], ACT.Square).then_inc(yc_sq, 1)
                for m in range(KC):
                    act.wait_ge(head_sum, 32 * ri + 24 + (m | 1) + 1)
                    own.up(nc.scalar.activation(rk_w[:, m, :], head_ps(m), ACT.Ln, bias=eps[:, 1:2], scale=1.0 / RN))
                    own.settle()
                    nc.scalar.activation(rk_w[:, m, :], rk_w[:, m, :], ACT.Exp, scale=-0.5).then_inc(y_rs, 1)
                for m in range(KC):
                    act.wait_ge(yg_ready, 8 * ri + m + 1)
                    nc.scalar.activation(x_hi[:, m, :], rk_k[:, m, :], ACT.Copy).then_inc(yg_hi, 1)
                for i in range(16, 20):
                    split_hi(Step(u + i + 2), width(u + i + 2))
                    square_y(s, 2 * i - 32)
                    square_y(s, 2 * i - 31)
                inverse_rms(2 * s + 1)

            def wkv_scalar(s):
                def halves(name, dst, src, reads_last=True):
                    wide = src.shape[2] == P
                    nc.scalar.activation(dst[0:64, :, 0:64], src[0:64, :, 0:64], ACT.Copy)
                    nc.scalar.activation(dst[64:P, :, 64:P], src[64:P, :, 64:P] if wide else src[64:P, :, :], ACT.Copy)\
                        .then_inc(wkv_act, 1)

                with act.Fori(0, 4) as c:
                    for half in range(2):
                        it = c * 2 + half
                        prs, cols = slice(4 * half, 4 * half + 4), bass.ds(c * 64, 64)

                        def vec(name):
                            act.wait_ge(wkv_vec, wkv_count(WKV_VEC, s, it, name))

                        def mul(name):
                            act.wait_ge(wkv_mul, wkv_count(WKV_MUL, s, it, name))

                        def out(dst, src, func=ACT.Copy, scale=1.0):
                            nc.scalar.activation(dst, src, func, scale=scale).then_inc(wkv_act, 1)

                        vec("begin")
                        out(ep_s, rk_l[:, prs, cols], ACT.Exp)
                        out(en_s, rk_l[:, prs, cols], ACT.Exp, -1.0)
                        vec("lm")
                        out(em_s, lm_s, ACT.Exp)
                        halves("v_b", v_b, rk_v[:, prs, cols])
                        vec("a")
                        halves("a_b", a_b, ar_s[:, :, 0:64])
                        vec("b")
                        halves("b_b", b_b, b_s)
                        ps = [wkv_ps[n].rearrange("p (a b) -> p a b", a=4) for n in range(7)]
                        vec("d")
                        halves("d_b", d_b, d_s)
                        vec("dt")
                        halves("dt_b", dt_b, dt_s)
                        vec("ot")
                        halves("ot_b", ot_b, ot_s)
                        mul("vt")
                        halves("vt_b", vt_b, ps[5])
                        nc.scalar.activation(vt_s[0:64], ps[5][0:64, :, 0:64], ACT.Copy)
                        out(vt_s[64:P], ps[5][64:P, :, 64:P])
                        mul("bt")
                        halves("bt_b", bt_b, ps[3])
                        mul("kt")
                        halves("kt_b", kt_b, ps[4])
                        vec("d2")
                        halves("d2_b", d2_b, d2_s)
                        vec("d2t")
                        halves("d2t_b", d2t_b, d2t_s)
                        mul("d4")
                        halves("d4_b", d4_b, part(1, 0))
                        vec("d4t")
                        halves("d4t_b", d4t_b, d4t_s)
                        mul("d8t")
                        halves("d8t_b", d8t_b, part(1, 0))
                        vec("td")
                        mul("t4")
                        halves("td_b", td_b, t_s)
                        mul("n1t")
                        halves("n1t_b", n1t_b, part(5, 0))
                        vec("e3")
                        halves("e_b", e_b, e_s)
                        vec("sa")
                        halves("sa_b", sa_b, sa_s)
                        mul("y")
                        out(rk_r[:, prs, cols], part(3, 0))
                        vec("state")
                        halves("st_b", st_b[half], st_s[half])
                        if half:
                            act.wait_ge(wkv_act, wkv_count(WKV_ACT, s, it, "st_b"))
                            mul("ds")
                            act.sem_inc(turn_over, 1)

            act.wait_ge(consts_in, CONSTS)
            act.wait_ge(const_set, 4)
            act.wait_ge(rope_arg, 2)
            nc.scalar.activation(sin_t[:, :], sin_t[:, :], ACT.Sin).then_inc(rope_done, 1)
            nc.scalar.activation(cos_t[:, :], cos_t[:, :], ACT.Sin).then_inc(rope_done, 1)
            act.wait_ge(lam_abs, 1)
            nc.scalar.activation(lru_c[:, 2, :], lru_c[:, 2, :], ACT.Exp, scale=-1.0).then_inc(lam_exp, 1)
            nc.scalar.activation(cond[:, :], cond[:, :], ACT.Silu).then_inc(cond_done, 1)
            split_hi(Step(0), width(0))
            split_hi(Step(1), width(1))
            u = 0
            for s in range(n_sub):
                {"ffn": ffn, "ret": retention, "lru": lru, "rwkv": rwkv}[kinds[s]](s, u)
                u += len(UNITS[kinds[s]])

        @block.vector
        def _(dve):
            own = Tally(dve, vec_own)

            def then(ins):
                own.up(ins)
                own.settle()

            def split_lo(step, w):
                if w is None:
                    return
                dve.wait_ge(hi_done, step.count(1))
                nc.vector.tensor_tensor(wt_lo[:, step.slot, 0:w], raw_w[:, step.slot, 0:w],
                                        wt_hi[:, step.slot, 0:w].bitcast(F32), ALU.subtract).then_inc(lo_done, 1)

            def ada(step, k):
                sl = step.slot
                dve.wait_ge(ada_in[sl], step.landed())
                ins = nc.vector.tensor_tensor_reduce(ada_w[:, sl, :], ada_w[:, sl, :], cond[:, :], 1.0, 0.0,
                                                     ALU.mult, ALU.add, mod_acc[:, sl:sl + 1])
                ins.then_inc(ada_used, 1)
                dve.wait_ge(ada_used, step.count(1))
                own.up(nc.vector.tensor_copy(mod[:, bass.ds(k, 1)], mod_acc[:, sl:sl + 1]))
                own.settle()

            def set_coef(s):
                layer, sub = PLAN[s]
                g = layer * 48 + sub * 16
                cf = coef[:, s % 2, :]
                w = 1.0 if sub == 1 else 0.5
                then(nc.vector.tensor_tensor(mod[:, :], mod[:, :], ada_b[:, layer * 72 + sub * 24:][:, 0:24], ALU.add))
                then(nc.vector.scalar_tensor_tensor(out=cf[:, 0:8], in0=mod[:, 8:16], scalar=1.0,
                                                    in1=norm_g[:, g:g + 8], op0=ALU.add, op1=ALU.mult))
                own.up(nc.vector.tensor_copy(cf[:, 8:16], mod[:, 0:8]))
                then(nc.vector.scalar_tensor_tensor(out=cf[:, 16:24], in0=mod[:, 16:24], scalar=w,
                                                    in1=norm_g[:, g + 8:g + 16], op0=ALU.mult, op1=ALU.mult))

            def pre_norm(s):
                cf = coef[:, s % 2, :]
                dve.wait_ge(rs_ready, 2 * s + 1)
                if s:
                    pass
                for m in range(KC):
                    own.up(nc.vector.tensor_tensor(scaled[:, m % 2, :], res[:, m, :], rstd[:, 0, :], ALU.mult))
                    own.settle()
                    nc.vector.tensor_scalar(hn[:, m, 1:T + 1], scaled[:, m % 2, :], cf[:, m:m + 1], cf[:, 8 + m:9 + m],
                                            ALU.mult, ALU.add).then_inc(hn_ready, 1)
                    if m and kinds[s] != "rwkv":
                        low_x(s, m - 1)
                if kinds[s] != "rwkv":
                    low_x(s, KC - 1)

            def low_x(s, m):
                dve.wait_ge(xh_ready, 8 * plain_index(s) + m + 1)
                nc.vector.tensor_tensor(x_lo[:, m, :], hn[:, m, 1:T + 1], x_hi[:, m, :].bitcast(F32),
                                        ALU.subtract).then_inc(x_ready, 1)

            def post_norm(s):
                cf = coef[:, s % 2, :]
                dve.wait_ge(rs_ready, 2 * s + 2)
                for m in range(KC):
                    then(nc.vector.scalar_tensor_tensor(out=scaled[:, m % 2, :], in0=ybuf[:, m, :],
                                                        scalar=cf[:, 16 + m:17 + m], in1=rstd[:, 1, :],
                                                        op0=ALU.mult, op1=ALU.mult))
                    nc.vector.tensor_tensor(res[:, m, :], res[:, m, :], scaled[:, m % 2, :], ALU.add).then_inc(res_ready, 1)

            def take_y(s, m, bank):
                nc.vector.tensor_copy(ybuf[:, bass.ds(m, 1), :], out_ps[:, bank:bank + 1, 0:T]).then_inc(y_ready, 1)

            def ffn(s, u):
                f = ffn_index(s)
                more = s + 1 < n_sub
                a0 = 24 * (s + 1)
                bank0 = uses[s] % 2

                def pair(step, astep, j, w0, w1):
                    for b, w in ((0, w0), (1, w1)):
                        split_lo(step + (2 + b), w)
                        sl = (step + b).slot
                        if not (isinstance(j, int) and j + b < 2 and f == 0):
                            dve.wait_ge(hl_ready, j + (FJ * f + b - 1))
                        dve.wait_ge(silu_done, j + (FJ * f + b + 1))
                        nc.vector.tensor_tensor(h_raw[:, sl, :], gate_act[:, sl, :], out_ps[:, bank0 ^ b, T:2 * T],
                                                ALU.mult).then_inc(h_ready, 1)
                        if more:
                            ada(astep + b, j + b)
                        else:
                            dve.wait_ge(h_ready, j + (FJ * f + b + 1))
                        dve.wait_ge(hh_ready, j + (FJ * f + b + 1))
                        nc.vector.tensor_tensor(h_lo[:, bass.ds(j + b, 1), :], h_raw[:, sl:sl + 1, :],
                                                h_hi[:, bass.ds(j + b, 1), :].bitcast(F32), ALU.subtract).then_inc(hl_ready, 1)

                pair(Step(u), Step(a0), 0, UNIT, UNIT)
                for i in own.loop(FJ // 2 - 2, 2 if more else 0):
                    pair(Step(u + 2, i), Step(a0 + 2, i), i * 2 + 2, UNIT, UNIT)
                pair(Step(u + FJ - 2), Step(a0 + FJ - 2), FJ - 2, WOUT, WOUT)
                v = u + FJ
                q = uses[s] + FJ

                def quad(step, m, last=False):
                    for b in range(2):
                        for g in range(2):
                            k = 2 * b + g
                            split_lo(step + (2 + k), width(v + 16 + k - 2) if last and k >= 2 else WOUT)
                        dve.wait_ge(unit_mul, (step + (2 * b + 1)).count(1))
                        take_y(s, m + b, (q + b) % 2)

                for i in own.loop(3, 0):
                    quad(Step(v, i, 4), i * 2)
                quad(Step(v + 12), 6, True)
                if more:
                    for k in range(2):
                        ada(Step(a0 + FJ + k), FJ + k)
                    set_coef(s + 1)
                post_norm(s)

            def ada_some(s, first, n):
                if s + 1 < n_sub:
                    for k in range(first, first + n):
                        ada(Step(24 * (s + 1) + k), k)

            def out_proj(s, u, q, w, ada_first=None):
                n = u + 8
                with_ada = ada_first is not None and s + 1 < n_sub
                a0 = 24 * (s + 1) + (ada_first or 0)

                def two(step, astep, m, w0, w1):
                    for b, wb in ((0, w0), (1, w1)):
                        split_lo(step + (2 + b), wb)
                        if with_ada:
                            ada(astep + b, m + (ada_first + b))
                        dve.wait_ge(unit_mul, (step + b).count(1))
                        take_y(s, m + b, (q + b) % 2)

                for i in own.loop(3, 2 if with_ada else 0):
                    two(Step(u, i), Step(a0, i), i * 2, w, w)
                two(Step(u + 6), Step(a0 + 6), 6, width(n), width(n + 1))

            def retention(s, u):
                q = uses[s]
                cos_b = cos_t[:, :].unsqueeze(1).broadcast_to([P, 2, T])
                sin_b = sin_t[:, :].unsqueeze(1).broadcast_to([P, 2, T])
                by_cos = ret_o[:, 0, :].rearrange("p (c t) -> p c t", c=2)
                by_sin = ret_o[:, 1, :].rearrange("p (c t) -> p c t", c=2)
                dve.wait_ge(rope_done, 2)
                for side, dst in enumerate((ybuf, sq)):
                    for i in own.loop(2, 4):
                        for b in range(2):
                            step = Step(u + 4 * side + b, i)
                            split_lo(step + 2, UNIT)
                            dve.wait_ge(unit_mul, step.count(1))
                            x = out_ps[:, (q + b) % 2, :].rearrange("p (c t) -> p c t", c=2)
                            own.up(nc.vector.tensor_tensor(by_cos, x, cos_b, ALU.mult))
                            then(nc.vector.tensor_tensor(by_sin, x, sin_b, ALU.mult))
                            nc.vector.tensor_tensor(dst[:, bass.ds(i * 4 + 2 * b, 1), :], by_cos[:, 0:1, :], by_sin[:, 1:2, :],
                                                    ALU.subtract)
                            nc.vector.tensor_tensor(dst[:, bass.ds(i * 4 + (2 * b + 1), 1), :], by_sin[:, 0:1, :], by_cos[:, 1:2, :],
                                                    ALU.add).then_inc(kq_ready, 1)
                            dve.wait_ge(kq_ready, i * 2 + (4 * side + b + 1))
                more = s + 1 < n_sub
                v = u + 8
                a0 = 24 * (s + 1)
                for i in own.loop(4, 2 if more else 0):
                    for b in range(2):
                        split_lo(Step(v + 2 + b, i), UNIT)
                        if more:
                            ada(Step(a0 + b, i), i * 2 + b)
                g = v + 8
                dve.wait_ge(decay_in, 16)
                for i in range(8):
                    split_lo(Step(g + i + 2), width(g + i + 2))
                    ada_some(s, 8 + i, 1)
                    if i < 4:
                        if i == 0:
                            for h in range(RET_H):
                                dve.wait_ge(score_mul, h + 1)
                                nc.vector.tensor_tensor(ret_s[:, h, :], mix_ps[:, h, 0:384], ret_s[:, h, :], ALU.mult).then_inc(score_ready, 1)
                        for t in range(2):
                            bank = 2 * (i % 2) + t
                            dve.wait_ge(o_mul, 2 * i + 2)
                            then(nc.vector.bn_stats(stats[:, t, :], mix_ps[:, bank, :]))
                            own.up(nc.vector.bn_aggr(mv[:, t, :], stats[:, t, :]))
                            then(nc.vector.tensor_copy(ret_v[:, t, 512 * i:512 * i + 512], mix_ps[:, bank, :]))
                            nc.vector.tensor_copy(ret_mv[:, :, 2 * i + t], mv[:, t, :]).then_inc(var_ready, 1)
                    elif i > 4:
                        ret_head(i - 5)
                ret_head(3)
                out_proj(s, g + 8, q, UNIT, 16)
                if more:
                    set_coef(s + 1)
                post_norm(s)

            def ret_head(h):
                if h == 0:
                    dve.wait_ge(rs_ready_o, 1)
                for t in range(2):
                    n = 2 * h + t
                    nc.vector.tensor_scalar(ret_v[:, t, 512 * h:512 * h + 512], ret_v[:, t, 512 * h:512 * h + 512],
                                            ret_mv[:, 0, n:n + 1], ret_rs[:, n:n + 1], ALU.subtract, ALU.mult).then_inc(o_ready, 1)
                for t in range(2):
                    n = 2 * h + t
                    dve.wait_ge(turned, n + 1)
                    if t == 0:
                        dve.wait_ge(g_ready, 2 * h + 2)
                    nc.vector.tensor_tensor(ret_o[:, t, :].rearrange("p (c t) -> p c t", c=4),
                                            mix_ps[:, n % 4, :].rearrange("p (c t) -> p c t", c=4),
                                            ret_g[:, 4 * h:4 * h + 4, t * P:t * P + P], ALU.mult).then_inc(r_ready, 1)
                for t in range(2):
                    n = 2 * h + t
                    dve.wait_ge(rh_ready, n + 1)
                    nc.vector.tensor_tensor(h_lo[:, 4 * h:4 * h + 4, t * P:t * P + P], ret_o[:, t, :].rearrange("p (c t) -> p c t", c=4),
                                            h_hi[:, 4 * h:4 * h + 4, t * P:t * P + P].bitcast(F32), ALU.subtract).then_inc(rl_ready, 1)

            def lru(s, u):
                q = uses[s]
                nc.vector.memset(lru_xb[:, :, 0:3], 0.0).then_inc(lru_pad, 1)
                for i in range(5):
                    split_lo(Step(u + i + 2), UNIT)
                    ada_some(s, i, 1)
                for i in range(5, 10):
                    split_lo(Step(u + i + 2), UNIT)
                    ada_some(s, i, 1)
                    for m in (2 * i - 10, 2 * i - 9):
                        if m % 2 == 0:
                            dve.wait_ge(xb_ready, m // 2 + 1)
                        then(nc.vector.tensor_scalar(lru_xc[:, m, :], lru_xb[:, m, 0:T], lru_p[:, m:m + 1], lru_p[:, 40 + m:41 + m],
                                                     ALU.mult, ALU.add))
                        for w in range(1, CONV_W):
                            ins = nc.vector.scalar_tensor_tensor(out=lru_xc[:, m, :], in0=lru_xb[:, m, w:w + T],
                                                                 scalar=lru_p[:, 10 * w + m:10 * w + m + 1], in1=lru_xc[:, m, :],
                                                                 op0=ALU.mult, op1=ALU.add)
                            if w < CONV_W - 1:
                                then(ins)
                        ins.then_inc(conv_ready, 1)
                    for m in (2 * i - 10, 2 * i - 9):
                        dve.wait_ge(xch_ready, m + 1)
                        nc.vector.tensor_tensor(h_lo[:, m, :], lru_xc[:, m, :], h_hi[:, m, :].bitcast(F32), ALU.subtract).then_inc(xcl_ready, 1)
                for h in range(5):
                    c = slice(2 * h, 2 * h + 2)
                    dve.wait_ge(gate_ready, 4 * h + 2)
                    nc.vector.tensor_tensor(lru_ig[:, c, :], lru_ig[:, c, :], lru_xc[:, c, :], ALU.mult)
                    dve.wait_ge(tanh_ready, 2 * h + 2)
                    then(nc.vector.tensor_scalar(lru_d[:, c, :], lru_t[:, c, :], 1.0, None, ALU.add))
                    then(nc.vector.reciprocal(lru_d[:, c, :], lru_d[:, c, :]))
                    nc.vector.scalar_tensor_tensor(out=lru_t[:, c, :], in0=lru_t[:, c, :], scalar=2.0, in1=lru_d[:, c, :],
                                                   op0=ALU.mult, op1=ALU.mult).then_inc(m_ready, 1)
                    if h % 2 or h == 4:
                        split_lo(Step(u + 12 + h // 2), width(u + 12 + h // 2))
                        ada_some(s, 10 + h // 2, 1)
                ada_some(s, 13, 3)
                dve.wait_ge(a_ready, LC)
                for h in range(5):
                    c = slice(2 * h, 2 * h + 2)
                    dve.wait_ge(beta_ready, h + 1)
                    then(nc.vector.tensor_tensor(lru_ig[:, c, :], lru_ig[:, c, :], lru_t[:, c, :], ALU.mult))
                    for m in (2 * h, 2 * h + 1):
                        ins = nc.vector.tensor_tensor_scan(lru_xc[:, m, :], lru_rg[:, m, :], lru_ig[:, m, :], 0.0, ALU.mult, ALU.add)
                    then(ins)
                    if h == 0:
                        dve.wait_ge(gb_ready, 5)
                    nc.vector.tensor_tensor(lru_xc[:, c, :], lru_xc[:, c, :], lru_gb[:, c, :], ALU.mult).then_inc(hs_ready, 1)
                    if h:
                        hs_low(h - 1)
                hs_low(4)
                out_proj(s, u + 13, q + 20, LRU_OUT, 16)
                if s + 1 < n_sub:
                    set_coef(s + 1)
                post_norm(s)

            def rwkv(s, u):
                layer = PLAN[s][0]
                q, ri, vres = uses[s], rwkv_index(s), layer > 0
                par = rk_p[:, layer // 3, :]
                more = s + 1 < n_sub

                def param(k):
                    return par[:, 8 * k:8 * k + 8].unsqueeze(2).broadcast_to([P, KC, T])

                n_mix = [48 * ri]

                def mix_x(count):
                    for _ in range(count):
                        n = n_mix[0]
                        j, m = n % 48 // 8, n % 8
                        nc.vector.scalar_tensor_tensor(out=scaled[:, n % 2, :], in0=sq[:, m, :],
                                                       scalar=par[:, 64 + 8 * MU_AT[j] + m:65 + 8 * MU_AT[j] + m],
                                                       in1=hn[:, m, 1:T + 1], op0=ALU.mult, op1=ALU.add).then_inc(xj_raw, 1)
                        if _:
                            mix_low(n - 1)
                        n_mix[0] += 1
                    mix_low(n_mix[0] - 1)

                def mix_low(n):
                    j, m = n % 48 // 8, n % 8
                    dve.wait_ge(xj_hi, n + 1)
                    nc.vector.tensor_tensor(mixed_x(j)[1][:, m, :], scaled[:, n % 2, :], mixed_x(j)[0][:, m, :].bitcast(F32),
                                            ALU.subtract).then_inc(xj_ready, 1)
                    dve.wait_ge(xj_ready, n + 1)

                def lora_low(js):
                    for j in js:
                        dve.wait_ge(lora_hi, 4 * ri + j + 1)
                        nc.vector.tensor_tensor(h_lo[:, 16 + j, :], lora_raw[:, j, :], h_hi[:, 16 + j, :].bitcast(F32),
                                                ALU.subtract).then_inc(lora_ready, 1)

                dve.wait_ge(hn_ready, 8 * s + 8)
                for m in range(KC):
                    own.up(nc.vector.tensor_tensor(sq[:, m, :], hn[:, m, 0:T], hn[:, m, 1:T + 1], ALU.subtract))
                own.settle()
                mix_x(8)
                for i in range(4):
                    split_lo(Step(u + i + 2), UNIT)
                    mix_x(4)
                split_lo(Step(u + 6), UNIT)
                ada_some(s, 0, 2)
                lora_low((0, 1))
                for i in range(5, 9):
                    split_lo(Step(u + i + 2), UNIT)
                    mix_x(4)
                    ada_some(s, i - 3, 1)
                for i in range(9, 13):
                    split_lo(Step(u + i + 2), UNIT)
                    mix_x(2)
                    ada_some(s, 6 + 2 * (i - 9), 2)
                split_lo(Step(u + 15), UNIT)
                ada_some(s, 14, 2)
                lora_low((2, 3))
                ada_some(s, 16, 4)
                split_lo(Step(u + 16), UNIT)
                ada_some(s, 20, 4)
                if more:
                    set_coef(s + 1)
                rd = reads_before(s)
                dve.wait_ge(proj_read, rd + 22)
                nc.vector.tensor_tensor(rk_kk, rk_k, param(3), ALU.mult).then_inc(kk_in, 1)
                dve.wait_ge(kk_in, ri + 1)
                then(nc.vector.scalar_tensor_tensor(out=rk_l, in0=rk_a, scalar=-1.0, in1=param(4), op0=ALU.add, op1=ALU.mult))
                then(nc.vector.scalar_tensor_tensor(out=rk_k, in0=rk_l, scalar=1.0, in1=rk_k, op0=ALU.add, op1=ALU.mult))
                then(nc.vector.tensor_scalar(rk_w, rk_w, -DECAY_RATE, None, ALU.mult))
                carry = wkv_c[:, 6:10, :].rearrange("p a b -> p (a b)")
                for m in range(KC):
                    own.up(nc.vector.tensor_tensor_scan(rk_l[:, m, :], carry, rk_w[:, m, :], 0.0, ALU.mult, ALU.add))
                split_lo(Step(u + 17), UNIT)
                if vres:
                    dve.wait_ge(proj_read, rd + 30)
                    dve.wait_ge(v_back, 16)
                    then(nc.vector.tensor_tensor(ybuf, ybuf, rk_v, ALU.subtract))
                    then(nc.vector.tensor_tensor(ybuf, ybuf, rk_sv, ALU.mult))
                    then(nc.vector.tensor_tensor(rk_v, rk_v, ybuf, ALU.add))
                else:
                    dve.wait_ge(proj_read, rd + 26)
                    dve.wait_ge(v_kept, 16)
                for m in range(KC):
                    dve.wait_ge(head_sum, 32 * ri + (m | 1) + 1)
                    ins = nc.vector.tensor_scalar(rk_bonus[:, m, :], head_ps(m), 1e-24, None, ALU.max)
                ins.then_inc(kk_norm, 1)
                dve.wait_ge(kk_root, ri + 1)
                then(nc.vector.reciprocal(rk_bonus, rk_bonus))
                then(nc.vector.tensor_tensor(rk_kk, rk_kk, rk_bonus, ALU.mult))
                own.up(nc.vector.tensor_tensor(rk_a, rk_a, rk_kk, ALU.mult))
                then(nc.vector.tensor_tensor(rk_bonus, rk_r, rk_k, ALU.mult))
                nc.vector.tensor_tensor(rk_bonus, rk_bonus, param(5), ALU.mult).then_inc(rk_prod, 1)
                for m in range(KC):
                    dve.wait_ge(head_sum, 32 * ri + 8 + (m | 1) + 1)
                    ins = nc.vector.tensor_tensor(rk_bonus[:, m, :], head_ps(m), rk_v[:, m, :], ALU.mult)
                then(ins)
                for t in (a_b, b_b, k_b, v_b, d_b, dt_b, ot_b, m2_b, bt_b, kt_b, vt_b, *st_b, *st_s):
                    ins = nc.vector.memset(t, 0.0)
                then(ins)
                wkv_vector(s)
                for m in range(KC):
                    dve.wait_ge(head_sum, 32 * ri + 16 + (m | 1) + 1)
                    nc.vector.scalar_tensor_tensor(out=rk_k[:, m, :], in0=head_ps(m), scalar=-1.0 / RN, in1=rk_r[:, m, :],
                                                   op0=ALU.mult, op1=ALU.add).then_inc(yc_ready, 1)
                for m in range(KC):
                    dve.wait_ge(y_rs, 8 * ri + m + 1)
                    then(nc.vector.tensor_tensor(rk_k[:, m, :], rk_k[:, m, :], rk_w[:, m, :], ALU.mult))
                    then(nc.vector.tensor_scalar(rk_k[:, m, :], rk_k[:, m, :], par[:, 48 + m:49 + m], par[:, 56 + m:57 + m],
                                                 ALU.mult, ALU.add))
                    then(nc.vector.tensor_tensor(rk_k[:, m, :], rk_k[:, m, :], rk_bonus[:, m, :], ALU.add))
                    nc.vector.tensor_tensor(rk_k[:, m, :], rk_k[:, m, :], rk_g[:, m, :], ALU.mult).then_inc(yg_ready, 1)
                    if m:
                        yg_low(ri, m - 1)
                yg_low(ri, KC - 1)
                for i in range(16, 20):
                    split_lo(Step(u + i + 2), width(u + i + 2))
                    dve.wait_ge(unit_mul, u + i + 1)
                    for c in range(2):
                        nc.vector.tensor_copy(ybuf[:, 2 * i - 32 + c, :], out_ps[:, (q + 14 + i) % 2, c * T:c * T + T]).then_inc(y_ready, 1)
                post_norm(s)

            def yg_low(ri, m):
                dve.wait_ge(yg_hi, 8 * ri + m + 1)
                nc.vector.tensor_tensor(x_lo[:, m, :], rk_k[:, m, :], x_hi[:, m, :].bitcast(F32), ALU.subtract).then_inc(yg_lo, 1)

            def wkv_vector(s):
                def mask(n):
                    return wkv_c[:, n:n + 1, :].broadcast_to([P, 4, 64])

                TT = nc.vector.tensor_tensor
                dve.sem_inc(turn_over, 1)
                for c in own.loop(4, 0):
                    for half in range(2):
                        it = c * 2 + half
                        prs, cols = slice(4 * half, 4 * half + 4), bass.ds(c * 64, 64)

                        def act_(name):
                            dve.wait_ge(wkv_act, wkv_count(WKV_ACT, s, it, name))

                        def mul(name):
                            dve.wait_ge(wkv_mul, wkv_count(WKV_MUL, s, it, name))

                        def vec(name):
                            dve.wait_ge(wkv_vec, wkv_count(WKV_VEC, s, it, name))

                        def done(ins):
                            ins.then_inc(wkv_vec, 1)

                        if half:
                            dve.wait_ge(wkv_act, wkv_count(WKV_ACT, s, c * 2, "st_b"))
                            dve.wait_ge(wkv_mul, wkv_count(WKV_MUL, s, c * 2, "ds"))
                        else:
                            dve.wait_ge(turn_over, c + (5 * rwkv_index(s) + 1))
                        dve.sem_inc(wkv_vec, 1)
                        done(TT(lm_s, rk_l[:, prs, cols], rk_w[:, prs, cols], ALU.subtract))
                        act_("ep")
                        done(TT(ar_s[:, :, 64:P], rk_r[:, prs, cols], ep_s, ALU.mult))
                        act_("em")
                        done(nc.vector.scalar_tensor_tensor(out=ar_s[:, :, 0:64], in0=rk_kk[:, prs, cols], scalar=-1.0, in1=em_s,
                                                            op0=ALU.mult, op1=ALU.mult))
                        done(TT(b_s, rk_a[:, prs, cols], en_s, ALU.mult))
                        TT(k_b[0:64, :, 0:64], rk_k[0:64, prs, cols], en_s[0:64], ALU.mult)
                        done(TT(k_b[64:P, :, 64:P], rk_k[64:P, prs, cols], en_s[64:P], ALU.mult))
                        mul("m1t")
                        done(TT(dt_s, part(2, 0), mask(1), ALU.mult))
                        done(TT(ot_s, part(2, 0), mask(2), ALU.mult))
                        mul("m13")
                        m13 = wkv_ps[0].rearrange("p (a b) -> p a b", a=4)
                        m24 = wkv_ps[1].rearrange("p (a b) -> p a b", a=4)
                        done(TT(d_s, m13[:, :, 0:64], mask(0), ALU.mult))
                        vec("d")
                        done(TT(t_s, d_s, mask(5), ALU.add))
                        done(TT(m3_s, m13[:, :, 64:P], mask(4), ALU.mult))
                        mul("m24")
                        TT(m2_b[0:64, :, 0:64], m24[0:64, :, 0:64], mask(3)[0:64], ALU.mult)
                        done(TT(m2_b[64:P, :, 64:P], m24[64:P, :, 0:64], mask(3)[64:P], ALU.mult))
                        done(TT(m4_s, m24[:, :, 64:P], mask(4), ALU.mult))
                        mul("d2")
                        done(nc.vector.tensor_copy(d2_s, part(6, 0)))
                        mul("d2t")
                        done(nc.vector.tensor_copy(d2t_s, part(2, 0)))
                        mul("t2")
                        done(TT(t_s, part(0, 0), t_s, ALU.add))
                        mul("d4t")
                        done(nc.vector.tensor_copy(d4t_s, part(6, 0)))
                        mul("t3")
                        vec("t2")
                        done(TT(t_s, part(2, 0), t_s, ALU.add))
                        mul("t4")
                        vec("t3")
                        done(TT(t_s, part(0, 0), t_s, ALU.add))
                        mul("n1")
                        done(nc.vector.tensor_copy(n1_s, part(6, 0)))
                        done(TT(e_s, part(6, 0), mask(5), ALU.add))
                        mul("n2")
                        done(nc.vector.tensor_copy(n2_s, part(2, 0)))
                        vec("e1")
                        done(TT(e_s, part(2, 0), e_s, ALU.add))
                        mul("n3")
                        vec("e2")
                        done(TT(e_s, part(0, 0), e_s, ALU.add))
                        mul("g")
                        done(nc.vector.tensor_copy(g_s, part(1, 0)))
                        mul("h")
                        done(nc.vector.tensor_copy(h_s, part(6, 0)))
                        mul("sa")
                        done(nc.vector.tensor_copy(sa_s, part(2, 0)))
                        mul("ds")
                        done(TT(st_s[half], part(4, 0), st_s[half], ALU.add))
                        vec("sum")
                        done(TT(st_s[half], st_s[half], ep_s[:, :, 63:64].broadcast_to([P, 4, 64]), ALU.mult))

            def hs_low(h):
                c = slice(2 * h, 2 * h + 2)
                dve.wait_ge(hsh_ready, h + 1)
                nc.vector.tensor_tensor(h_lo[:, c, :], lru_xc[:, c, :], h_hi[:, c, :].bitcast(F32), ALU.subtract).then_inc(hsl_ready, 1)

            def rope_arguments():
                turn = 2 * np.pi
                c1 = 6.28125
                c2 = float((np.float32(turn - c1).view(np.uint32) & np.uint32(0xFFFFF000)).view(np.float32))
                c3 = turn - c1 - c2
                ang = sq[:, 1, :]
                then(nc.vector.tensor_copy(sq[:, 2, :], sq[:, 0, :].bitcast(I32)))
                then(nc.vector.tensor_scalar(ang, sq[:, 2, :], freq[:, 0:1], None, ALU.mult))
                for dst, turns, shift in ((sin_t, 0.0, 0.0), (cos_t, 0.25, turn / 4)):
                    n = sq[:, 3, :]
                    then(nc.vector.tensor_scalar(n, ang, 1.0 / turn, turns, ALU.mult, ALU.add))
                    then(nc.vector.tensor_scalar(n, n, ROUND, None, ALU.add))
                    then(nc.vector.tensor_scalar(n, n, -ROUND, None, ALU.add))
                    then(nc.vector.scalar_tensor_tensor(out=dst[:, :], in0=n, scalar=-c1, in1=ang, op0=ALU.mult, op1=ALU.add))
                    then(nc.vector.scalar_tensor_tensor(out=dst[:, :], in0=n, scalar=-c2, in1=dst[:, :], op0=ALU.mult, op1=ALU.add))
                    then(nc.vector.scalar_tensor_tensor(out=dst[:, :], in0=n, scalar=-c3, in1=dst[:, :], op0=ALU.mult, op1=ALU.add))
                    if shift:
                        then(nc.vector.tensor_scalar(dst[:, :], dst[:, :], shift, None, ALU.add))
                    nc.vector.tensor_scalar(dst[:, :], dst[:, :], PI_LOW, -PI_LOW, ALU.min, ALU.max).then_inc(rope_arg, 1)

            def decay_rates():
                lam = lru_p[:, 70:80]
                neg, mag, z, p = (lru_c[:, n, :] for n in (0, 2, 3, 4))
                then(nc.vector.tensor_scalar(neg, lam, -1.0, None, ALU.mult))
                nc.vector.tensor_tensor(mag, lam, neg, ALU.max).then_inc(lam_abs, 1)
                dve.wait_ge(lam_exp, 1)
                then(nc.vector.tensor_scalar(z, mag, 2.0, None, ALU.add))
                then(nc.vector.reciprocal(z, z))
                then(nc.vector.tensor_tensor(z, z, mag, ALU.mult))
                then(nc.vector.tensor_tensor(mag, z, z, ALU.mult))
                then(nc.vector.tensor_scalar(p, mag, 1.0 / 17, None, ALU.mult))
                for k in (15, 13, 11, 9, 7, 5, 3):
                    then(nc.vector.scalar_tensor_tensor(out=p, in0=p, scalar=1.0 / k, in1=mag, op0=ALU.add, op1=ALU.mult))
                then(nc.vector.scalar_tensor_tensor(out=p, in0=p, scalar=1.0, in1=z, op0=ALU.add, op1=ALU.mult))
                then(nc.vector.tensor_scalar(neg, neg, 0.0, None, ALU.max))
                then(nc.vector.scalar_tensor_tensor(out=p, in0=p, scalar=2.0, in1=neg, op0=ALU.mult, op1=ALU.add))
                own.up(nc.vector.tensor_scalar(lru_c[:, 1, :], p, -8.0, None, ALU.mult))
                then(nc.vector.tensor_scalar(lru_c[:, 0, :], p, 8.0, None, ALU.mult))

            then(nc.vector.memset(head_ones[:, :], 0.0))
            nc.vector.memset(head_ones[0:64, 0:64], 1.0)
            nc.vector.memset(head_ones[64:P, 64:P], 1.0)
            nc.vector.memset(eps[:, 2:3], HEAD_EPS)
            nc.vector.memset(ones[:, :], 1.0).then_inc(const_set, 1)
            nc.vector.memset(hn[:, :, 0:1], 0.0).then_inc(const_set, 1)
            nc.vector.memset(eps[:, 0:1], NORM_EPS).then_inc(const_set, 1)
            nc.vector.memset(eps[:, 1:2], GN_EPS).then_inc(const_set, 1)
            dve.wait_ge(consts_in, CONSTS)
            rope_arguments()
            decay_rates()
            split_lo(Step(0), width(0))
            split_lo(Step(1), width(1))
            dve.wait_ge(cond_done, 1)
            ada(Step(0), 0)
            ada(Step(1), 1)
            for i in own.loop(11, 2):
                for b in range(2):
                    ada(Step(2 + b, i), i * 2 + (2 + b))
            set_coef(0)
            u = 0
            for s in range(n_sub):
                pre_norm(s)
                {"ffn": ffn, "ret": retention, "lru": lru, "rwkv": rwkv}[kinds[s]](s, u)
                u += len(UNITS[kinds[s]])

        @block.tensor
        def _(pe):
            def product(dst, slot, blocks):
                return product_part(dst, slot, blocks, True, True)

            def product_part(dst, slot, blocks, first, last, before=None):
                for n, (col, hi, lo) in enumerate(blocks):
                    if before:
                        before(n)
                    wh, wl = wt_hi[:, slot, col:col + P], wt_lo[:, slot, col:col + P]
                    nc.tensor.matmul(dst, wh, hi, start=first and n == 0, stop=False)
                    nc.tensor.matmul(dst, wh, lo, start=False, stop=False)
                    mm = nc.tensor.matmul(dst, wl, hi, start=False, stop=last and n == len(blocks) - 1)
                return mm

            def sum_squares(m, first, last):
                mm = nc.tensor.matmul(sum_ps[:, 0:T], ones[:, :], sq[:, m, :] if isinstance(m, int) else
                                      sq[:, bass.ds(m, 1), :], start=first, stop=last)
                if last:
                    mm.then_inc(sum_done, 1)

            def pre_norm(s):
                if s:
                    pe.wait_ge(rs_ready, 2 * s)
                for m in range(KC):
                    pe.wait_ge(sq_ready, 16 * s + m + 1)
                    sum_squares(m, m == 0, m == KC - 1)

            def y_sum(s, m, first=False, last=False):
                if isinstance(m, int):
                    pe.wait_ge(sq_ready, 16 * s + 9 + m)
                else:
                    pe.wait_ge(sq_ready, m + (16 * s + 9))
                if first:
                    pe.wait_ge(rs_ready, 2 * s + 1)
                sum_squares(m, first, last)

            def ffn(s, u):
                f = ffn_index(s)
                pre_norm(s)
                bank0 = uses[s] % 2

                def pair(step, j):
                    for b in range(2):
                        st = step + b
                        pe.wait_ge(lo_done, st.count(1))
                        if not (isinstance(j, int) and j + b < 2):
                            pe.wait_ge(h_ready, j + (FJ * f + b - 1))
                        elif s:
                            pass
                        for half in range(2):
                            blocks = [(k * 2 * P + half * P, x_hi[:, k, :], x_lo[:, k, :]) for k in range(KC)]
                            wait_x = None
                            if isinstance(j, int) and j + b + half == 0:
                                def wait_x(k):
                                    pe.wait_ge(x_ready, 8 * plain_index(s) + k + 1)
                            mm = product_part(out_ps[:, bank0 ^ b, half * T:half * T + T], st.slot, blocks, True, True, wait_x)
                        mm.then_inc(unit_mul, 1)

                if s:
                    pe.wait_ge(y_ready, 8 * s)
                pair(Step(u), 0)
                with pe.Fori(1, FJ // 2) as i:
                    pair(Step(u, i), i * 2)
                v = u + FJ
                q = uses[s] + FJ

                def quad(step, m):
                    for b in range(2):
                        bank = (q + b) % 2
                        if not (isinstance(m, int) and m == 0):
                            pe.wait_ge(y_ready, m + (8 * s + b - 1))
                        for g in range(2):
                            st = step + (2 * b + g)
                            pe.wait_ge(lo_done, st.count(1))
                            if isinstance(m, int) and m == 0 and b == 0:
                                pe.wait_ge(hl_ready, FJ * f + HALF_K * (g + 1))
                                pe.wait_ge(h_ready, FJ * f + FJ - 1 + g)
                            blocks = [(k * P, h_hi[:, g * HALF_K + k, :], h_lo[:, g * HALF_K + k, :]) for k in range(HALF_K)]
                            product_part(out_ps[:, bank, 0:T], st.slot, blocks, g == 0, g == 1).then_inc(unit_mul, 1)
                        if isinstance(m, int):
                            if b:
                                y_sum(s, m, m == 0, False)
                            elif m:
                                y_sum(s, m - 1)
                        else:
                            y_sum(s, m + (b - 1))

                quad(Step(v), 0)
                with pe.Fori(1, 4) as i:
                    quad(Step(v, i, 4), i * 2)
                y_sum(s, 7, False, True)

            def chunks(*where):
                hi, lo, n = where
                return [(hi[:, k, :], lo[:, k, :]) for k in range(n)]

            def out_proj(s, u, q, n_k, bank_free):
                def two(step, m):
                    for b in range(2):
                        if isinstance(m, int):
                            bank_free(b)
                        else:
                            pe.wait_ge(y_ready, m + (8 * s + b - 1))
                        pe.wait_ge(lo_done, (step + b).count(1))
                        blocks = [(k * P, h_hi[:, k, :], h_lo[:, k, :]) for k in range(n_k)]
                        product(out_ps[:, (q + b) % 2, 0:T], (step + b).slot, blocks).then_inc(unit_mul, 1)
                        if isinstance(m, int):
                            if b:
                                y_sum(s, 0, True)
                        else:
                            y_sum(s, m + (b - 1))

                two(Step(u), 0)
                with pe.Fori(1, 4) as i:
                    two(Step(u, i), i * 2)
                y_sum(s, 7, False, True)

            def in_unit(step, bank, first=None):
                pe.wait_ge(lo_done, step.count(1))
                for half in range(2):
                    blocks = [(k * 2 * P + half * P, x_hi[:, k, :], x_lo[:, k, :]) for k in range(KC)]
                    mm = product_part(out_ps[:, bank, half * T:half * T + T], step.slot, blocks, True, True, first if half == 0 else None)
                mm.then_inc(unit_mul, 1)

            def x_part(s):
                def wait_x(k):
                    pe.wait_ge(x_ready, 8 * plain_index(s) + k + 1)
                return wait_x

            def retention(s, u):
                q = uses[s]
                pre_norm(s)
                if s:
                    pe.wait_ge(y_ready, 8 * s)
                in_unit(Step(u), q % 2, x_part(s))
                in_unit(Step(u + 1), (q + 1) % 2)
                with pe.Fori(1, 4) as i:
                    for b in range(2):
                        pe.wait_ge(kq_ready, i * 2 + (b - 1))
                        in_unit(Step(u + b, i), (q + b) % 2)
                v = u + 8

                def value_unit(step, bank):
                    pe.wait_ge(lo_done, step.count(1))
                    for t in range(2):
                        tok = slice(t * P, t * P + P)
                        dst = out_ps[:, bank, t * T:t * T + T]
                        for k in range(KC):
                            wh, wl = (w[:, step.slot, k * 2 * P:(k + 1) * 2 * P] for w in (wt_hi, wt_lo))
                            nc.tensor.matmul(dst, x_hi[:, k, tok], wh, start=k == 0, stop=False)
                            nc.tensor.matmul(dst, x_hi[:, k, tok], wl, start=False, stop=False)
                            mm = nc.tensor.matmul(dst, x_lo[:, k, tok], wh, start=False, stop=k == KC - 1)
                    mm.then_inc(unit_mul, 1)

                for b in range(2):
                    pe.wait_ge(kq_ready, 7 + b)
                    value_unit(Step(v + b), (q + b) % 2)
                with pe.Fori(1, 4) as i:
                    for b in range(2):
                        pe.wait_ge(v_ready, i * 2 + (b - 1))
                        value_unit(Step(v + b, i), (q + b) % 2)
                for h in range(RET_H):
                    for keys, queries, col in ((0, 0, 0), (P, P, T)):
                        for c in range(2):
                            mm = nc.tensor.matmul(mix_ps[:, h, col:col + T - queries], ybuf[:, 2 * h + c, keys:keys + P],
                                                  sq[:, 2 * h + c, queries:T], start=c == 0, stop=c == 1)
                    mm.then_inc(score_mul, 1)
                g = v + 8
                for i in range(8):
                    if i < 2:
                        pe.wait_ge(v_ready, 7 + i)
                    else:
                        pe.wait_ge(g_ready, i - 1)
                    in_unit(Step(g + i), (q + i) % 2)
                    if i < 4:
                        if i == 0:
                            pe.wait_ge(score_ready, RET_H)
                            pe.wait_ge(v_ready, 8)
                        else:
                            pe.wait_ge(var_ready, 2 * i - 2)
                        b0 = 2 * (i % 2)
                        vals = [ret_v[:, t, 512 * i:512 * i + 512] for t in range(2)]
                        nc.tensor.matmul(mix_ps[:, b0, :], ret_s[:, i, 0:P], vals[0], start=True, stop=True).then_inc(o_mul, 1)
                        nc.tensor.matmul(mix_ps[:, b0 + 1, :], ret_s[:, i, P:2 * P], vals[0], start=True, stop=False)
                        nc.tensor.matmul(mix_ps[:, b0 + 1, :], ret_s[:, i, 2 * P:3 * P], vals[1], start=False, stop=True).then_inc(o_mul, 1)
                    elif i > 4:
                        turn_head(i - 5)
                turn_head(3)

                def bank_free(b):
                    pe.wait_ge(g_ready, 7 + b)
                    if b == 0:
                        pe.wait_ge(rl_ready, 8)
                out_proj(s, g + 8, q, 16, bank_free)

            def turn_head(h):
                if h >= 2:
                    pe.wait_ge(r_ready, 2 * h - 2)
                for t in range(2):
                    n = 2 * h + t
                    pe.wait_ge(o_ready, n + 1)
                    for c in range(4):
                        at = 512 * h + c * P
                        mm = nc.tensor.transpose(mix_ps[:, n % 4, c * P:c * P + P], ret_v[:, t, at:at + P], ident[:, :])
                    mm.then_inc(turned, 1)

            def lru(s, u):
                q = uses[s]
                pre_norm(s)
                if s:
                    pe.wait_ge(y_ready, 8 * s)
                for i in range(10):
                    if 2 <= i < 7:
                        pe.wait_ge(xb_ready, i - 1)
                    elif i >= 7:
                        pe.wait_ge(gb_ready, i - 6)
                    in_unit(Step(u + i), (q + i) % 2, x_part(s) if i == 0 else None)
                for w in range(10):
                    h, g = w // 2, w % 2
                    step = Step(u + 10 + w // 4)
                    if w % 4 == 0:
                        pe.wait_ge(lo_done, step.count(1))
                    if g == 0:
                        pe.wait_ge(xcl_ready, 2 * h + 2)
                    if w < 2:
                        pe.wait_ge(gb_ready, 4 + w)
                    else:
                        pe.wait_ge(gate_ready, 2 * w - 2)
                    for half in range(2):
                        col = (w % 4) * 4 * P + half * 2 * P
                        blocks = [(col + k * P, h_hi[:, 2 * h + k, :], h_lo[:, 2 * h + k, :]) for k in range(2)]
                        mm = product(out_ps[:, (q + 10 + w) % 2, half * T:half * T + T], step.slot, blocks)
                    mm.then_inc(gate_mul, 1)
                    if w % 4 == 3 or w == 9:
                        pe.wait_ge(gate_mul, w + 1)
                        pe.sem_inc(unit_mul, 1)

                def bank_free(b):
                    pe.wait_ge(gate_ready, 18 + 2 * b)
                    if b == 0:
                        pe.wait_ge(hsl_ready, 5)
                out_proj(s, u + 13, q + 20, LC, bank_free)

            def rwkv(s, u):
                layer = PLAN[s][0]
                q, ri, vres = uses[s], rwkv_index(s), layer > 0
                rd, lm = reads_before(s), lora_before(s)
                used = [0]

                def bank():
                    n = used[0]
                    used[0] += 1
                    if n >= 2:
                        pe.wait_ge(proj_read, rd + n - 1)
                    return (q + n) % 2

                def have(j):
                    pe.wait_ge(xj_ready, 48 * ri + 8 * j + 8)

                def mixed_unit(step, b, j, first=None):
                    hi, lo = mixed_x(j)
                    pe.wait_ge(lo_done, step.count(1))
                    for half in range(2):
                        blocks = [(k * 2 * P + half * P, hi[:, k, :], lo[:, k, :]) for k in range(KC)]
                        mm = product_part(out_ps[:, b, half * T:half * T + T], step.slot, blocks, True, True, first if half == 0 else None)
                    mm.then_inc(unit_mul, 1)

                def rank_unit(step, b, js):
                    pe.wait_ge(lo_done, step.count(1))
                    for half, j in enumerate(js):
                        if j is None:
                            continue
                        have(j)
                        hi, lo = mixed_x(j)
                        blocks = [((8 * half + k) * P, hi[:, k, :], lo[:, k, :]) for k in range(KC)]
                        mm = product(out_ps[:, b, half * T:half * T + T], step.slot, blocks)
                    mm.then_inc(unit_mul, 1)

                def wide_unit(step, js):
                    pe.wait_ge(lo_done, step.count(1))
                    for half, j in enumerate(js):
                        if j is None:
                            continue
                        for c in range(4):
                            b = bank()
                            for k in range(2):
                                col = (8 * half + 2 * c + k) * P
                                mm = product(out_ps[:, b, k * T:k * T + T], step.slot, [(col, h_hi[:, 16 + j, :], h_lo[:, 16 + j, :])])
                            mm.then_inc(lora_mul, 1)
                            used_l[0] += 1
                    pe.wait_ge(lora_mul, lm + used_l[0])
                    pe.sem_inc(unit_mul, 1)

                used_l = [0]
                pre_norm(s)
                if s:
                    pe.wait_ge(y_ready, 8 * s)

                def wait_first(k):
                    pe.wait_ge(xj_ready, 48 * ri + k + 1)
                mixed_unit(Step(u), bank(), 0, wait_first)
                for i in range(1, 4):
                    mixed_unit(Step(u + i), bank(), 0)
                rank_unit(Step(u + 4), bank(), (0 if vres else None, 1))
                have(2)
                for i in range(5, 9):
                    mixed_unit(Step(u + i), bank(), 2)
                have(3)
                for i in range(9, 13):
                    mixed_unit(Step(u + i), bank(), 3)
                rank_unit(Step(u + 13), bank(), (4, 5))
                pe.wait_ge(lora_ready, 4 * ri + 4)
                wide_unit(Step(u + 14), (1, 2))
                wide_unit(Step(u + 15), (3, 0 if vres else None))

                def head_sums(src):
                    for m in range(KC):
                        nc.tensor.matmul(head_ps(m), head_ones[:, :], src[:, m, :], start=True, stop=True).then_inc(head_sum, 1)

                pe.wait_ge(kk_sq, ri + 1)
                head_sums(rk_bonus)
                pe.wait_ge(kk_norm, ri + 1)
                pe.wait_ge(rk_prod, ri + 1)
                head_sums(rk_bonus)
                pe.wait_ge(proj_read, rd + 26 + 4 * vres)
                wkv_tensor(s)
                pe.wait_ge(wkv_act, wkv_count(WKV_ACT, s, 7, "y"))
                head_sums(rk_r)
                for m in range(KC):
                    if m % 2 == 0:
                        pe.wait_ge(yc_ready, 8 * ri + m + 2)
                    pe.wait_ge(yc_sq, 8 * ri + m + 1)
                    nc.tensor.matmul(head_ps(m), head_ones[:, :], rk_w[:, m, :], start=True, stop=True).then_inc(head_sum, 1)
                pe.wait_ge(yg_lo, 8 * ri + KC)
                for i in range(16, 20):
                    b = (q + 14 + i) % 2
                    if i >= 18:
                        pe.wait_ge(y_ready, 8 * s + 2 * (i - 17))
                    step = Step(u + i)
                    pe.wait_ge(lo_done, step.count(1))
                    for half in range(2):
                        blocks = [(k * 2 * P + half * P, x_hi[:, k, :], x_lo[:, k, :]) for k in range(KC)]
                        mm = product(out_ps[:, b, half * T:half * T + T], step.slot, blocks)
                    mm.then_inc(unit_mul, 1)
                    if i > 16:
                        for m in (2 * i - 34, 2 * i - 33):
                            y_sum(s, m, m == 0)
                y_sum(s, 6)
                y_sum(s, 7, False, True)

            def wkv_tensor(s):
                with pe.Fori(0, 4) as c:
                    for half in range(2):
                        it = c * 2 + half

                        def vec(name):
                            pe.wait_ge(wkv_vec, wkv_count(WKV_VEC, s, it, name))

                        def act_(name):
                            pe.wait_ge(wkv_act, wkv_count(WKV_ACT, s, it, name))

                        def mm(dst, *terms):
                            for p in range(4):
                                for n, (lhs, rhs) in enumerate(terms):
                                    ins = nc.tensor.matmul(dst[:, p, :], lhs[:, p, :], rhs[:, p, :], start=n == 0,
                                                           stop=n == len(terms) - 1)
                            ins.then_inc(wkv_mul, 1)

                        def turn(bank, src):
                            for p in range(4):
                                ins = nc.tensor.transpose(wkv_ps[bank][:, p * P:p * P + P], src[:, p, :], ident[:, :])
                            ins.then_inc(wkv_mul, 1)

                        wide = [wkv_ps[n].rearrange("p (a b) -> p a b", a=4) for n in range(2)]
                        act_("a_b")
                        vec("b")
                        mm(part(2, 0), (a_b, b_s))
                        act_("b_b")
                        mm(wide[0], (b_b, ar_s))
                        vec("k_b")
                        mm(wide[1], (k_b, ar_s))
                        turn(5, v_b)
                        turn(3, b_b)
                        turn(4, k_b)
                        act_("dt_b")
                        vec("d")
                        mm(part(6, 0), (dt_b, d_s))
                        act_("d_b")
                        mm(part(2, 0), (d_b, dt_s))
                        act_("d2t_b")
                        vec("m3")
                        vec("t1")
                        mm(part(0, 0), (d2t_b, t_s))
                        vec("d2")
                        mm(part(1, 0), (d2t_b, d2_s))
                        vec("m4")
                        vec("d2t")
                        mm(part(6, 0), (d2_b, d2t_s))
                        vec("t2")
                        act_("d4t_b")
                        mm(part(2, 0), (d4t_b, t_s))
                        vec("d4t")
                        mm(part(1, 0), (d4_b, d4t_s))
                        vec("t3")
                        act_("d8t_b")
                        mm(part(0, 0), (d8t_b, t_s))
                        vec("td")
                        act_("ot_b")
                        mm(part(6, 0), (ot_b, t_s))
                        act_("td_b")
                        mm(part(5, 0), (td_b, ot_s))
                        vec("n1")
                        act_("n1t_b")
                        mm(part(2, 0), (n1t_b, n1_s))
                        vec("n2")
                        mm(part(0, 0), (n1t_b, n2_s))
                        act_("vt_s")
                        vec("m2_b")
                        mm(part(1, 0), (a_b, st_s[half]), (m2_b, vt_s))
                        vec("g")
                        mm(part(6, 0), (td_b, g_s))
                        vec("h")
                        act_("e_b")
                        mm(part(2, 0), (e_b, h_s))
                        act_("kt_b")
                        act_("sa_b")
                        mm(part(3, 0), (sa_b, m3_s), (vt_b, m4_s), (st_b[half], ar_s[:, :, 64:P]))
                        vec("sa")
                        mm(part(4, 0), (bt_b, sa_s), (kt_b, vt_s))

            pe.wait_ge(const_set, 4)
            pe.wait_ge(consts_in, CONSTS)
            u = 0
            for s in range(n_sub):
                {"ffn": ffn, "ret": retention, "lru": lru, "rwkv": rwkv}[kinds[s]](s, u)
                u += len(UNITS[kinds[s]])


def blocks_of(w, n):
    k, c = w.shape
    return w.reshape(k // P, P, n, c // n).transpose(2, 1, 0, 3).reshape(n, P, -1)


def rope_freq():
    return (np.float32(1.0) / np.float32(10000.0) ** np.linspace(0.0, 1.0, P, dtype=np.float32)).astype(np.float32)[:, None]


def retention_decay():
    gamma = 1.0 - 2.0 ** (-5.0 - np.arange(RET_H))
    lag = np.arange(T)[None, :] - np.arange(P)[:, None]
    first = np.where((lag >= 0)[:, None, :], gamma[None, :, None] ** np.maximum(lag, 0)[:, None, :], 0.0) / 16.0
    return np.concatenate([first, first[:, :, :P]], 2).astype(np.float32)


def rwkv_units(a):
    def first(w):
        w = np.pad(w, ((0, 0), (0, P - w.shape[1])))
        return w.reshape(KC, P, P).transpose(1, 0, 2).reshape(P, KC * P)

    def second(w):
        return np.pad(w, ((0, P - w.shape[0]), (0, 0)))

    layers = []
    for j in range(2):
        v1 = a["rwkv_v1"][0] if j else np.zeros((D, 32), np.float32)
        v2 = a["rwkv_v2"][0] if j else np.zeros((32, D), np.float32)
        w = a["rwkv_w_rkv"][j]
        layers += [blocks_of(w[2], 4), np.concatenate([first(v1), first(a["rwkv_w1"][j])], 1)[None],
                   blocks_of(w[1], 4), blocks_of(w[0], 4),
                   np.concatenate([first(a["rwkv_a1"][j]), first(a["rwkv_g1"][j])], 1)[None],
                   np.concatenate([second(a["rwkv_w2"][j]), second(a["rwkv_a2"][j])], 1)[None],
                   np.concatenate([second(a["rwkv_g2"][j]), second(v2)], 1)[None], blocks_of(a["rwkv_w_o"][j], 4)]
    return np.concatenate(layers).reshape(2, 20, P, UNIT)


def rwkv_params(a):
    v0 = np.concatenate([np.zeros((1, D), np.float32), a["rwkv_v0"]])
    rows = [a["rwkv_w0"], a["rwkv_a0"], v0, a["rwkv_k_k"], a["rwkv_k_a"], a["rwkv_r_k"].reshape(2, D), a["rwkv_ln_w"],
            a["rwkv_ln_b"]] + [a["rwkv_mu"][:, j] for j in range(6)]
    return np.stack(rows, 1).reshape(2, 112, P).transpose(2, 0, 1)


def wkv_constants():
    r, c = np.arange(64)[:, None], np.arange(64)[None, :]
    same = r // 16 == c // 16
    masks = [(r < c) & same, (r > c) & same, (r > c) & ~same, r < c, r <= c, r == c]
    carry = np.ones((P, 4, 64), np.float32)
    carry[:, :, 0] = 0.0
    m = np.stack([np.tile(x, (2, 1)) for x in masks], 1).astype(np.float32)
    return np.concatenate([m, carry], 1)


def kernel(**inputs):
    import concourse.bacc as _bacc
    from concourse.bass_utils import run_bass_kernel_spmd as _run

    a = {k: np.asarray(v) for k, v in inputs.items()}
    F = 2 * DEPTH
    ret, lru_in = a["ret_w_in"][0], a["lru_w_in"][0]
    gates = a["lru_gate_w"][0].reshape(2, 5, 2, P, 2, P).transpose(1, 3, 0, 4, 2, 5).reshape(5, P, 8 * P)
    lru_gates = np.concatenate([gates, np.zeros((1, P, 8 * P), np.float32)]).reshape(3, 2, P, 8 * P)
    lru_gates = lru_gates.transpose(0, 2, 1, 3).reshape(3, P, UNIT)
    arrays = {
        "x_t": a["x"][0].T.reshape(KC, P, T).transpose(1, 0, 2),
        "c_row": a["c"],
        "ada_t": a["ada_w"].transpose(0, 2, 1).reshape(DEPTH * 72, P, D),
        "ada_bt": a["ada_b"].reshape(DEPTH * 72, P).T,
        "norm_gt": a["norm_g"].reshape(DEPTH * 48, P).T,
        "w_in": a["ffn_w_in"].reshape(F, KC, P, 2, FJ, P).transpose(0, 4, 2, 1, 3, 5).reshape(F, FJ, P, UNIT),
        "w_out": a["ffn_w_out"].reshape(F, 2, HALF_K, P, KC, P).transpose(0, 4, 1, 3, 2, 5).reshape(F, 16, P, WOUT),
        "pos_row": a["positions"],
        "rope_freq": rope_freq(),
        "ret_decay": retention_decay(),
        "ident_c": np.eye(P, dtype=np.float32),
        "ret_w": blocks_of(np.concatenate([ret[:, D:2 * D], ret[:, :D], ret[:, 2 * D:]], 1), 24),
        "ret_wo": blocks_of(a["ret_w_o"][0], 8),
        "lru_w": np.concatenate([blocks_of(np.concatenate([lru_in[:, LW:], lru_in[:, :LW]], 1), 10), lru_gates]),
        "lru_wo": blocks_of(a["lru_w_o"][0], 8),
        "rwkv_w": rwkv_units(a),
        "rwkv_par": rwkv_params(a),
        "wkv_const": wkv_constants(),
        "lru_par": np.concatenate([a["lru_conv_w"][0], a["lru_conv_b"], a["lru_gate_b"][0].reshape(2, LW), a["lru_lambda"]])
        .reshape(8 * LC, P).T,
    }
    nc = _bacc.Bacc("TRN2", target_bir_lowering=False, num_devices=1)
    arrays = {k: np.ascontiguousarray(v) for k, v in arrays.items()}
    args = [nc.dram_tensor(k, v.shape, mybir.dt.from_np(v.dtype), kind="ExternalInput").ap() for k, v in arrays.items()]
    args.append(nc.dram_tensor("v_keep", (P, KC, T), F32, kind="Internal").ap())
    out = nc.dram_tensor("out", (P, KC, T), F32, kind="ExternalOutput").ap()
    build_program(nc, *args, out)
    r = _run(nc, [arrays], core_ids=[0])
    got = r.results[0]["out"]
    return got.transpose(2, 1, 0).reshape(1, T, D)
```
